# Optimizing a Trainium2 kernel written in Bass

```python
import math
import jax, jax.numpy as jnp
from jax import lax
import numpy as np

D_MODEL = 1024
BATCH = 1
SEQ = 128
DEPTH = 1
DEC_BATCH = 1
DEC_SEQ = 512
PAST_LEN = 128

GRID_W = 64
POOL_WIDTH = 512
POOL_GROUPS = 4
POOL_GROUP_DIM = POOL_WIDTH // POOL_GROUPS
POOL_WINDOWS = (2, 4, 8, 16)
N_RET_HEADS = 4
RET_DK = 128
RET_DV = 256
RET_QK_WIDTH = N_RET_HEADS * RET_DK
RET_V_WIDTH = N_RET_HEADS * RET_DV
IN_WIDTH = POOL_WIDTH + 2 * RET_QK_WIDTH + 2 * RET_V_WIDTH
RET_CHUNK = 128
N_BRANCHES = 2
N_EXPERTS = 16
EXPERT_FF = 2816
EC_CAPACITY_FACTOR = 2
ROPE_BASE = 10000.0
EPS = 1e-6

kernel_name = "hybrid_pool_retention_ec_moe_diffusion_step"

def rms_norm(x, g):
    xf = x.astype(jnp.float32)
    y = xf * lax.rsqrt(jnp.mean(xf * xf, axis=-1, keepdims=True) + EPS)
    return (y * g.astype(jnp.float32)).astype(x.dtype)

def adaln_params(cond, w, b):
    return jnp.split(jax.nn.silu(cond) @ w + b, 6, axis=-1)

def rope_tables(L):
    rows = L // GRID_W
    row = jnp.repeat(jnp.arange(rows, dtype=jnp.float32), GRID_W)
    col = jnp.tile(jnp.arange(GRID_W, dtype=jnp.float32), rows)
    nf = RET_DK // 4
    inv = ROPE_BASE ** (-jnp.arange(nf, dtype=jnp.float32) / nf)
    ang = jnp.concatenate([row[:, None] * inv, col[:, None] * inv], axis=-1)
    return jnp.cos(ang), jnp.sin(ang)

def apply_rope(x, cos, sin):
    xe, xo = x[..., 0::2], x[..., 1::2]
    return jnp.stack([xe * cos - xo * sin, xe * sin + xo * cos], axis=-1).reshape(x.shape)

def multiscale_pool(u, w_group, scale):
    B, L, _ = u.shape
    uf = u.astype(jnp.float32)
    cs = jnp.concatenate([jnp.zeros((B, 1, POOL_WIDTH), jnp.float32), jnp.cumsum(uf, axis=1)], axis=1)
    t = jnp.arange(L)
    pooled = []
    for gi, w in enumerate(POOL_WINDOWS):
        lo = jnp.clip(t - w // 2, 0, L)
        hi = jnp.clip(t + w // 2, 0, L)
        cnt = (hi - lo).astype(jnp.float32)[:, None]
        sl = slice(gi * POOL_GROUP_DIM, (gi + 1) * POOL_GROUP_DIM)
        csg = cs[:, :, sl]
        pooled.append((csg[:, hi] - csg[:, lo]) / cnt - uf[:, :, sl])
    p = jnp.stack(pooled, axis=2).astype(u.dtype)
    y = jnp.einsum('blgc,gcd->blgd', p, w_group).reshape(B, L, POOL_WIDTH)
    return y * scale

def retention_direction(q, k, v, log_gamma, s0, strict):
    B, H, L, _ = q.shape
    n = L // RET_CHUNK
    qc = q.reshape(B, H, n, RET_CHUNK, RET_DK)
    kc = k.reshape(B, H, n, RET_CHUNK, RET_DK)
    vc = v.reshape(B, H, n, RET_CHUNK, RET_DV)
    i = jnp.arange(RET_CHUNK, dtype=jnp.float32)
    diff = i[:, None] - i[None, :]
    valid = (diff > 0) if strict else (diff >= 0)
    intra_decay = jnp.where(valid, jnp.exp(log_gamma[:, None, None] * jnp.maximum(diff, 0.0)), 0.0)
    q_decay = jnp.exp(log_gamma[:, None] * (i + 1.0))
    k_decay = jnp.exp(log_gamma[:, None] * (RET_CHUNK - 1.0 - i))
    chunk_decay = jnp.exp(log_gamma * RET_CHUNK)[None, :, None, None]
    scores = jnp.einsum('bhncd,bhnmd->bhncm', qc, kc) * intra_decay[None, :, None]
    intra = jnp.einsum('bhncm,bhnmv->bhncv', scores, vc)
    kv = jnp.einsum('bhnmd,bhnmv->nbhdv', kc * k_decay[None, :, None, :, None], vc)

    def step(s, kv_n):
        return chunk_decay * s + kv_n, s

    s_final, s_start = lax.scan(step, s0, kv)
    inter = jnp.einsum('bhncd,nbhdv->bhncv', qc * q_decay[None, :, None, :, None], s_start)
    return (intra + inter).reshape(B, H, L, RET_DV), s_final

def retention_branch(z, decay_param, gn_gain, s0_f, s0_b, rope):
    B, L, _ = z.shape
    q, k, v, g = jnp.split(z, [RET_QK_WIDTH, 2 * RET_QK_WIDTH, 2 * RET_QK_WIDTH + RET_V_WIDTH], axis=-1)

    def heads(t, d):
        return t.astype(jnp.float32).reshape(B, L, N_RET_HEADS, d).transpose(0, 2, 1, 3)

    q = heads(q, RET_DK)
    k = heads(k, RET_DK) * (RET_DK ** -0.5)
    v = heads(v, RET_DV)
    if rope is not None:
        cos, sin = rope
        q = apply_rope(q, cos, sin)
        k = apply_rope(k, cos, sin)
    log_gamma = -jnp.exp(decay_param.astype(jnp.float32))
    o_f, s_f = retention_direction(q, k, v, log_gamma[0], s0_f.astype(jnp.float32), False)
    o_b, s_b = retention_direction(jnp.flip(q, 2), jnp.flip(k, 2), jnp.flip(v, 2), log_gamma[1],
                                   s0_b.astype(jnp.float32), True)
    o = o_f + jnp.flip(o_b, 2)
    mu = jnp.mean(o, axis=-1, keepdims=True)
    var = jnp.mean(jnp.square(o - mu), axis=-1, keepdims=True)
    o = (o - mu) * lax.rsqrt(var + EPS)
    o = o.transpose(0, 2, 1, 3).reshape(B, L, RET_V_WIDTH) * gn_gain.astype(jnp.float32)
    return (jax.nn.silu(g.astype(jnp.float32)) * o).astype(z.dtype), s_f, s_b

def expert_choice_moe(h, w_router, w_gate, w_up, w_down):
    B, L, D = h.shape
    cap = max(1, EC_CAPACITY_FACTOR * L // N_EXPERTS)
    aff = jax.nn.softmax(jnp.einsum('bld,de->ble', h, w_router).astype(jnp.float32), axis=-1)
    gate, idx = lax.top_k(jnp.swapaxes(aff, 1, 2), cap)
    xs = jax.vmap(lambda hb, ib: hb[ib])(h, idx)
    hid = jax.nn.silu(jnp.einsum('becd,edf->becf', xs, w_gate)) * jnp.einsum('becd,edf->becf', xs, w_up)
    out = jnp.einsum('becf,efd->becd', hid, w_down) * gate[..., None].astype(h.dtype)
    return jax.vmap(lambda ob, ib: jnp.zeros((L, D), ob.dtype).at[ib.reshape(-1)].add(ob.reshape(-1, D)))(out, idx)

def trunk_layer(x, cond, s0_f, s0_b, rope, p):
    shift1, scale1, gate1, shift2, scale2, gate2 = adaln_params(cond, p['w_ada'], p['b_ada'])
    h = rms_norm(x, p['norm1_g']) * (1.0 + scale1[:, None]) + shift1[:, None]
    z = jnp.einsum('bld,de->ble', h, p['w_in'])
    pool_y = multiscale_pool(z[..., :POOL_WIDTH], p['w_pool'], p['pool_scale']) @ p['w_pool_out']
    ret_h, s_f, s_b = retention_branch(z[..., POOL_WIDTH:], p['ret_decay'], p['ret_gn_g'], s0_f, s0_b, rope)
    ret_y = ret_h @ p['w_ret_out']
    gates = jax.nn.sigmoid(h @ p['w_branch_gate'] + p['b_branch_gate'])
    merged = gates[..., :D_MODEL] * pool_y + gates[..., D_MODEL:] * ret_y
    x = x + gate1[:, None] * (merged @ p['w_out'])
    h2 = rms_norm(x, p['norm2_g']) * (1.0 + scale2[:, None]) + shift2[:, None]
    x = x + gate2[:, None] * expert_choice_moe(h2, p['w_router'], p['w_exp_gate'], p['w_exp_up'], p['w_exp_down'])
    return x, s_f, s_b

def setup_inputs(seed: int = 0) -> dict:
    key = jax.random.key(seed)
    ks = jax.random.split(key, 26)
    f32 = jnp.float32
    nrm = lambda k, shape, s: jax.random.normal(k, shape, f32) * s
    gamma0 = 1.0 - 2.0 ** (-5.0 - np.arange(N_RET_HEADS, dtype=np.float32))
    decay_init = jnp.asarray(np.log(-np.log(gamma0)).astype(np.float32))
    return {
        "x_prompt": nrm(ks[0], (BATCH, SEQ, D_MODEL), 1.0),
        "x_sample": nrm(ks[1], (DEC_BATCH, DEC_SEQ, D_MODEL), 1.0),
        "c": nrm(ks[2], (DEC_BATCH, D_MODEL), 1.0),
        "state_ret": nrm(ks[3], (DEC_BATCH, DEPTH, 2, N_RET_HEADS, RET_DK, RET_DV), 1.0),
        "c_ctx": nrm(ks[4], (D_MODEL,), 1.0),
        "w_ada": nrm(ks[5], (DEPTH, D_MODEL, 6 * D_MODEL), 0.5 * D_MODEL ** -0.5),
        "b_ada": nrm(ks[6], (DEPTH, 6 * D_MODEL), 0.02),
        "norm1_g": 1.0 + nrm(ks[7], (DEPTH, D_MODEL), 0.02),
        "w_in": nrm(ks[8], (DEPTH, D_MODEL, IN_WIDTH), D_MODEL ** -0.5),
        "w_pool": nrm(ks[9], (DEPTH, POOL_GROUPS, POOL_GROUP_DIM, POOL_GROUP_DIM), POOL_GROUP_DIM ** -0.5),
        "pool_scale": 1.0 + nrm(ks[10], (DEPTH, POOL_WIDTH), 0.02),
        "w_pool_out": nrm(ks[11], (DEPTH, POOL_WIDTH, D_MODEL), POOL_WIDTH ** -0.5),
        "ret_decay": decay_init[None, None, :] + nrm(ks[12], (DEPTH, 2, N_RET_HEADS), 0.05),
        "ret_gn_g": 1.0 + nrm(ks[13], (DEPTH, RET_V_WIDTH), 0.02),
        "w_ret_out": nrm(ks[14], (DEPTH, RET_V_WIDTH, D_MODEL), RET_V_WIDTH ** -0.5),
        "w_branch_gate": nrm(ks[15], (DEPTH, D_MODEL, N_BRANCHES * D_MODEL), D_MODEL ** -0.5),
        "b_branch_gate": nrm(ks[16], (DEPTH, N_BRANCHES * D_MODEL), 0.02),
        "w_out": nrm(ks[17], (DEPTH, D_MODEL, D_MODEL), D_MODEL ** -0.5),
        "norm2_g": 1.0 + nrm(ks[18], (DEPTH, D_MODEL), 0.02),
        "w_router": nrm(ks[19], (DEPTH, D_MODEL, N_EXPERTS), D_MODEL ** -0.5),
        "w_exp_gate": nrm(ks[20], (DEPTH, N_EXPERTS, D_MODEL, EXPERT_FF), D_MODEL ** -0.5),
        "w_exp_up": nrm(ks[21], (DEPTH, N_EXPERTS, D_MODEL, EXPERT_FF), D_MODEL ** -0.5),
        "w_exp_down": nrm(ks[22], (DEPTH, N_EXPERTS, EXPERT_FF, D_MODEL), EXPERT_FF ** -0.5),
        "final_norm_g": 1.0 + nrm(ks[23], (D_MODEL,), 0.02),
    }

def reference(x_prompt, x_sample, c, state_ret, c_ctx, w_ada, b_ada, norm1_g, w_in, w_pool, pool_scale,
              w_pool_out, ret_decay, ret_gn_g, w_ret_out, w_branch_gate, b_branch_gate, w_out, norm2_g,
              w_router, w_exp_gate, w_exp_up, w_exp_down, final_norm_g):
    rope = rope_tables(x_sample.shape[1])
    zero_state = jnp.zeros((x_prompt.shape[0], N_RET_HEADS, RET_DK, RET_DV), jnp.float32)
    cond_ctx = c_ctx[None, :]
    xp, xs = x_prompt, x_sample
    layer_states = []
    for l in range(DEPTH):
        p = {
            'w_ada': w_ada[l], 'b_ada': b_ada[l], 'norm1_g': norm1_g[l], 'w_in': w_in[l],
            'w_pool': w_pool[l], 'pool_scale': pool_scale[l], 'w_pool_out': w_pool_out[l],
            'ret_decay': ret_decay[l], 'ret_gn_g': ret_gn_g[l], 'w_ret_out': w_ret_out[l],
            'w_branch_gate': w_branch_gate[l], 'b_branch_gate': b_branch_gate[l], 'w_out': w_out[l],
            'norm2_g': norm2_g[l], 'w_router': w_router[l], 'w_exp_gate': w_exp_gate[l],
            'w_exp_up': w_exp_up[l], 'w_exp_down': w_exp_down[l],
        }
        xp, s_f, s_b = trunk_layer(xp, cond_ctx, zero_state, zero_state, None, p)
        layer_states.append(jnp.stack([s_f, s_b], axis=1))
        xs, _, _ = trunk_layer(xs, c, state_ret[:, l, 0], state_ret[:, l, 1], rope, p)
    y_prompt = rms_norm(xp, final_norm_g)
    y_sample = rms_norm(xs, final_norm_g)
    new_state_ret = jnp.stack(layer_states, axis=1).astype(x_prompt.dtype)
    return (y_prompt, y_sample, new_state_ret)


_drawn_inputs = setup_inputs


def setup_inputs(seed=0):
    import zlib

    import numpy as np

    out = dict(_drawn_inputs(seed))
    spreads = {}
    factors = {'pool_scale': 8.0,
     'ret_gn_g': 8.0,
     'b_branch_gate': 8.0,
     'norm2_g': 8.0,
     'final_norm_g': 2.907}
    for name, (base, spread) in spreads.items():
        noise = np.random.default_rng([zlib.crc32(name.encode()), seed]).standard_normal(out[name].shape)
        drawn = base * np.exp(spread * noise) if base else spread * noise
        out[name] = __import__('jax').numpy.asarray(drawn.astype(out[name].dtype))
    for name, factor in factors.items():
        out[name] = (out[name] * factor).astype(out[name].dtype)
    return out
```

```python
import numpy as np
import concourse.bass as bass
from concourse import mybir
from contextlib import ExitStack

F32 = mybir.dt.float32
F32R = mybir.dt.float32r
I32 = mybir.dt.int32
U32 = mybir.dt.uint32
ALU = mybir.AluOpType
ACT = mybir.ActivationFunctionType
AX = mybir.AxisListType

P = 128
D = 1024
KT = D // P
L_S, L_P = 512, 128
NS = L_S // P
NT = NS + 1
T = L_S + L_P
HALF = T // 2
POOL_W = 512
WINDOWS = (2, 4, 8, 16)
H = 4
DK = 128
DV = 256
NE = 16
FF = 2816
C_S, C_P = 2 * L_S // NE, 2 * L_P // NE
CAP = C_S + C_P
GRID_W = 64
EPS = 1e-6

WB = 2048
RAW_T = 3
SPLIT_T = 2

FB = 352
NJ = FF // FB
DQ = 256
NQ = D // DQ
FT = FF // P
FTH = FT // 2
EB = KT * FB
assert EB == FTH * DQ
NB = 2 * NJ + 2 * NQ
RAW_E = 4
SPLIT_E = 2
TILE_EDGE = (0, 2, 5, 8, 11)
NG = NJ + 2

C_ID, C_DPL, C_DMI, C_QF, C_QB, C_KP, C_COS, C_SIN, C_EDGE, C_END = (
    0, 128, 256, 384, 512, 640, 642, 642 + 512, 642 + 1024, 642 + 1024 + 64)


def shape_tables():
    i = np.arange(P, dtype=np.float32)
    t = np.zeros((P, C_END), np.float32)
    t[:, C_ID:C_ID + P] = np.eye(P, dtype=np.float32)
    diff = i[None, :] - i[:, None]
    t[:, C_DPL:C_DPL + P] = np.maximum(diff, 0)
    t[:, C_DMI:C_DMI + P] = np.maximum(-diff, 0)
    t[:, C_QF:C_QF + P] = i[None, :] + 1
    t[:, C_QB:C_QB + P] = P - i[None, :]
    t[:, C_KP] = P - 1 - i
    t[:, C_KP + 1] = i
    nf = DK // 4
    inv = (np.float32(10000.0) ** (-np.arange(nf, dtype=np.float32) / np.float32(nf))).astype(np.float32)
    tok = np.arange(L_S)
    row, col = (tok // GRID_W).astype(np.float32), (tok % GRID_W).astype(np.float32)
    ang = np.concatenate([row[:, None] * inv, col[:, None] * inv], axis=-1).astype(np.float32)
    cos, sin = np.cos(ang), np.sin(ang)
    full_c = np.repeat(cos, 2, axis=1)
    full_s = np.stack([-sin, sin], axis=-1).reshape(L_S, DK)
    t[:, C_COS:C_COS + 512] = full_c.reshape(NS, P, DK).transpose(1, 0, 2).reshape(P, -1)
    t[:, C_SIN:C_SIN + 512] = full_s.reshape(NS, P, DK).transpose(1, 0, 2).reshape(P, -1)
    for g, w in enumerate(WINDOWS):
        for e in range(8):
            t[:, C_EDGE + 16 * g + e] = w / min(w, e + w // 2)
            t[:, C_EDGE + 16 * g + 8 + e] = w / min(w, 8 - e + w // 2)
    return t


def trunk_blocks():
    ada = [("ada", b) for b in range(24)]
    return (ada[:8] + [("q", 0), ("q", 1), ("k", 0), ("k", 1)] + [("v", b) for b in range(4)] + ada[8:]
            + [("g", b) for b in range(4)] + [("u", 0), ("u", 1)] + [("sr", b) for b in range(4)]
            + [("ro", b) for b in range(4)] + [("sp", b) for b in range(4)] + [("po", 0), ("po", 1)]
            + [("wo", b) for b in range(4)])


BLOCKS = trunk_blocks()
INDEX = {b: n for n, b in enumerate(BLOCKS)}
SPLITS = [b for b in BLOCKS if b[0] != "ada"]
SPLIT_AT = {b: m for m, b in enumerate(SPLITS)}


def acc_units():
    out = []
    for b in SPLITS[:8]:
        out += [(b + (lt,), "act") for lt in range(NT)]
    for h in range(H):
        out += [(("kvf", h, lt), "state") for lt in (0, 1, 2)] + [(("kvb", h, lt), "state") for lt in (3, 2, 1)]
        out += [(("kvf", h, 4), "dve"), (("kvb", h, 4), "dve")]
        for lt in range(NT + 1):
            if lt < NT:
                out.append((("sc", h, lt), "dve"))
            if lt:
                out.append((("o", h, lt - 1), "act"))
    for b in SPLITS[8:]:
        if b == ("sp", 0):
            out += [(("pg", g, f), "product") for g in range(4) for f in range(2)]
        if b[0] == "wo":
            out += [(b + (lt,), "dve") for lt in range(NT)]
        else:
            engine = "act" if b[0] in ("g", "u", "sr", "sp") else "dve"
            n = 4 if b[0] == "po" else 2
            out += [(b + (c, f), engine) for c in range(n) for f in range(2)]
    return out


def tr_units():
    out = [(("vec", 0, 0), "act")] + [(("h", lt, i), "h") for lt in range(NT) for i in range(2)]
    for b in SPLITS[:4]:
        out += [(("t", b[0], b[1], lt), "act") for lt in range(NT)]
    for h in range(H):
        if h:
            out += [(("on", h - 1, lt), "act") for lt in range(NT)]
    out += [(("ada", 0, 0), "act")]
    out += [(("on", H - 1, lt), "act") for lt in range(NT)]
    for lt in range(NT):
        out += [(("h2", lt, 0), "act"), (("h2", lt, 1), "act"), (("lg", lt, 0), "dve"), (("af", lt, 0), "act")]
    out += [(("ix", 0, 0), "dve"), (("ga", 0, 0), "dve")]
    return out


class Plan:

    def __init__(self, units, banks):
        self.at = {u: i for i, (u, _) in enumerate(units)}
        self.engine = [e for _, e in units]
        self.banks = banks
        self.n = len(units)

    def bank(self, u):
        return self.banks[self.at[u] % len(self.banks)]

    def full(self, u):
        return self.at[u] + 1

    def previous(self, u):
        i = self.at[u] - len(self.banks)
        if i < 0:
            return None
        n = sum(e == self.engine[i] for e in self.engine[:i + 1])
        if self.engine[i] == "h":
            n *= 4
        if self.engine[i] == "product":
            n += 16
        return self.engine[i], n


ACC = Plan(acc_units(), (0, 1, 2, 3, 4))
TR = Plan(tr_units(), (5, 6))


def build(nc, x_prompt, x_sample, c, state_ret, c_ctx, w_ada, b_ada, norm1_g, w_in, w_pool, pool_scale,
          w_pool_out, ret_decay, ret_gn_g, w_ret_out, w_branch_gate, b_branch_gate, w_out, norm2_g,
          w_router, w_exp_gate, w_exp_up, w_exp_down, final_norm_g, tables, y_prompt, y_sample, new_state):
    ctx = ExitStack()
    with ctx:
        base = 16512

        def at(name, offset, shape, dt=F32):
            return nc.alloc_sbuf_tensor_at(name, shape, dt, offset=base + offset)

        A, X, CC, RT, HT, M0 = 0, 45056, 65536, 116736, 141312, 174080
        act_hi, act_lo = at("act_hi", A, [P, KT, T], F32R), at("act_lo", A + 20480, [P, KT, T], F32R)
        cos_t, sin_t = at("cos_t", A + 40960, [P, NS, DK]), at("sin_t", A + 43008, [P, NS, DK])
        x_in = at("x_in", X, [P, NT, D])
        o_t = at("o_t", X, [P, KT, T])
        mix = at("mix", X, [P, KT, T])
        x2 = at("x2", X, [P, NT, D])
        x_sq = at("x_sq", CC, [P, D])
        xn = at("xn", CC + 4096, [P, 2, D])
        q_rope = at("q_rope", X + 2048, [P, 2, 256])
        probs = at("probs", A + 40960, [P, 2, P])
        rope_tmp = at("rope_tmp", X, [P, 256])
        h_tmp = at("h_tmp", CC + 12288, [P, 2, 512])
        q_t, k_t = at("q_t", CC, [P, H, T]), at("k_t", CC + 10240, [P, H, T])
        k_n = at("k_n", CC + 20480, [P, NT, H * DK])
        v_n = at("v_n", CC + 30720, [P, NT, H * DV])
        ret_hi, ret_lo = at("ret_hi", CC, [P, KT, T], F32R), at("ret_lo", CC + 20480, [P, KT, T], F32R)
        pooled = at("pooled", CC + 40960, [P, 4, T])
        py_hi, py_lo = at("py_hi", CC, [P, 4, T], F32R), at("py_lo", CC + 10240, [P, 4, T], F32R)
        sig_p = at("sig_p", CC + 20480, [P, KT, T])
        raw_t = at("raw_t", RT, [P, RAW_T, WB])
        wt_hi, wt_lo = at("wt_hi", HT, [P, SPLIT_T, WB], F32R), at("wt_lo", HT + 16384, [P, SPLIT_T, WB], F32R)

        place = [M0]

        def misc(name, shape, dt=F32, alias=None):
            size = int(np.prod(shape[1:])) * 4
            size += -size % 32
            if alias is not None:
                return at(name, alias, shape, dt)
            place[0] += size
            return at(name, place[0] - size, shape, dt)

        ident = misc("ident", [P, P])
        ada_t = misc("ada_t", [P, 48, 2])
        vec_rows = at("vec_rows", CC, [N_VEC, P])
        cols = misc("cols", [P, N_VEC])
        n1g, n2g, gng, pscale, bbg, bada = (cols[:, a:b] for a, b in (
            (16, 24), (24, 32), (32, 40), (40, 44), (44, 60), (60, 108)))
        scond = misc("scond", [P, 2, KT])
        gs1 = misc("gs1", [P, KT, 2])
        lgam = misc("lgam", [P, 2, H])
        kdec = misc("kdec", [P, 2, H])
        cdec = misc("cdec", [P, 2, H])
        kpow = misc("kpow", [P, 2])
        edge = misc("edge", [P, 4, 16])
        mv = misc("mv", [P, NT, 2])
        small = misc("small", [P, 64])
        wr_sb = misc("wr_sb", [P, KT, NE])
        wp_sb = misc("wp_sb", [P, 4, P])
        dead = place[0]
        mask = misc("mask", [P, H, P])
        qfp, qbp = misc("qfp", [P, H, P]), misc("qbp", [P, H, P])
        qk_raw = misc("qk_raw", [P, 2, 256])
        kf, kb = misc("kf", [P, NT, P]), misc("kb", [P, NT, P])
        qf, qb = misc("qf", [P, NS, P]), misc("qb", [P, NS, P])
        s0 = misc("s0", [P, 2, 2, DV])
        states = misc("states", [P, 6, DV])
        o_raw = place[0]
        pows = misc("pows", [P, 4, P], alias=o_raw)
        o_raw = misc("o_raw", [P, NT, DV])
        assert base + place[0] <= 229344, place[0]
        pool_a = at("pool_a", dead, [P, 2, 544])
        gtmp = at("gtmp", dead + 4352, [P, 2, HALF])
        rtmp = at("rtmp", dead + 6912, [P, 2, HALF])
        g1_b = at("g1_b", dead + 9472, [P, 2, D])
        gs2_b = at("gs2_b", dead + 17664, [P, 2, D])
        adar = at("adar", dead + 25856, [96, P])
        assert dead + 25856 + 512 <= 229344 - base
        h2 = at("h2", RT, [P, 2, D])
        h2_t = at("h2_t", RT + 8192, [P, 2, D])
        x2_sq = at("x2_sq", RT + 16384, [P, D])
        sh2_b = at("sh2_b", HT + 20480, [P, 2, D])
        aff = at("aff", RT + 20480, [P, 2, NE])
        aff_t = at("aff_t", HT, [NE, 2, T])
        top_v = at("top_v", HT + 5120, [NE, CAP])
        top_i = at("top_i", HT + 5504, [NE, CAP], U32)
        top_f = at("top_f", HT + 5888, [NE, CAP])
        idx_all = at("idx_all", HT + 6272, [CAP, NE], I32)
        gate_all = at("gate_all", HT + 6336, [CAP, NE])
        raw_e = at("raw_e", CC, [P, RAW_E, EB])
        we_hi, we_lo = at("we_hi", A, [P, SPLIT_E, EB], F32R), at("we_lo", A + 22528, [P, SPLIT_E, EB], F32R)
        xs_hi, xs_lo = at("xs_hi", X, [P, KT, CAP], F32R), at("xs_lo", X + 2560, [P, KT, CAP], F32R)
        x_rows = at("x_rows", X + 5120, [CAP, D])
        out_rows = at("out_rows", X + 9216, [CAP, D])
        g2_rows = at("g2_rows", X + 13312, [CAP, D])
        silu_g = at("silu_g", X + 17408, [CAP, 2, FB])
        hid = at("hid", HT + 6400, [CAP, 4 * FB])
        hd_hi, hd_lo = at("hd_hi", RT, [P, FT, CAP], F32R), at("hd_lo", RT + 7040, [P, FT, CAP], F32R)
        gate_cur = at("gate_cur", HT + 12160, [CAP, 1])
        idx_gather = at("idx_gather", HT + 12192, [CAP, 1], I32)
        idx_scatter = at("idx_scatter", HT + 12224, [CAP, 1], I32)
        fg_b = at("fg_b", dead + 26400, [P, D])
        assert dead + 26400 + 4096 <= 229344 - base, dead
        y_tile = at("y_tile", CC, [P, NT, D])
        y_sq = at("y_sq", CC + 20480, [P, D])

        bank = [ctx.enter_context(nc.psum_tensor(f"bank{i}", [P, 512], F32)) for i in range(8)]
        ada_ps = bank[7]

        h2_dram = nc.dram_tensor("h2_scratch", (T, D), F32, kind="Internal").ap()
        acc_dram = nc.dram_tensor("acc_scratch", (T, D), F32, kind="Internal").ap()
        ada_dram = nc.dram_tensor("ada_scratch", (96, P), F32, kind="Internal").ap()

        def sem(name):
            return ctx.enter_context(nc.semaphore(name))

        s_x = [sem(f"s_x{i}") for i in range(NT)]
        s_cond, s_const, s_decay, s_s0 = sem("s_cond"), sem("s_const"), sem("s_decay"), [sem("s_s0a"), sem("s_s0b")]
        s_pow = sem("s_pow")
        w_landed = [sem(f"w_landed{i}") for i in range(RAW_T)]
        w_hi_done, w_lo_done, ada_done = sem("w_hi_done"), sem("w_lo_done"), sem("ada_done")
        acc_full = sem("acc_full")
        acc_read = {"act": sem("acc_read_act"), "dve": sem("acc_read_dve")}
        tr_full = sem("tr_full")
        tr_read = {"act": sem("tr_read_act"), "dve": sem("tr_read_dve")}
        s_scond, s_ada0, s_ada, s_gs = sem("s_scond"), sem("s_ada0"), sem("s_ada"), sem("s_gs")
        s_x2, s_fg = sem("s_x2done"), sem("s_fg")
        s_ms, s_sqrt, s_rstd, s_xn = sem("s_ms"), sem("s_sqrt"), sem("s_rstd"), sem("s_xn")
        s_htmp, s_hhi, s_hlo = sem("s_htmp"), sem("s_hhi"), sem("s_hlo")
        tr_read["h"] = s_htmp
        s_rope = sem("s_rope")
        s_exp, s_lgam, s_marg, s_tab = sem("s_exp"), sem("s_lgam"), sem("s_marg"), sem("s_tab")
        s_kdec, s_qdec = sem("s_kdec"), sem("s_qdec")
        s_state, s_outst, s_stdma = sem("s_state"), sem("s_outst"), sem("s_stdma")
        s_mv, s_osq, s_on = sem("s_mv"), sem("s_osq"), sem("s_on")
        s_adar, s_adaw, s_bc = sem("s_adar"), sem("s_adaw"), sem("s_bc")
        s_gsil, s_gmul, s_ghi, s_glo = sem("s_gsil"), sem("s_gmul"), sem("s_ghi"), sem("s_glo")
        acc_read["state"], acc_read["product"] = s_state, s_gmul
        s_pool, s_pooled = sem("s_pool"), sem("s_pooled")
        s_x2in = [sem(f"s_x2in{i}") for i in range(NT)]
        s_mixfree = sem("s_mixfree")
        dve_step, act_step = sem("dve_step"), sem("act_step")
        s_h2, s_h2w, s_acc = sem("s_h2"), [sem(f"s_h2w{i}") for i in range(NT)], sem("s_acc")
        s_rmax, s_rexp, s_aff = sem("s_rmax"), sem("s_rexp"), sem("s_aff")
        s_top, s_idx = sem("s_top"), sem("s_idx")
        e_landed = [sem(f"e_landed{i}") for i in range(RAW_E)]
        e_hi, e_lo, e_used = sem("e_hi"), sem("e_lo"), sem("e_used")
        e_silu, e_hid, e_tr, e_tr_hi, e_tr_split = (sem(n) for n in ("e_silu", "e_hid", "e_tr", "e_tr_hi", "e_tr_split"))
        s_hold = sem("s_hold")
        e_out, e_idx, e_gath, s_g2 = sem("e_out"), sem("e_idx"), sem("e_gath"), sem("s_g2")
        s_fin, s_y, s_out = [sem(f"s_fin{i}") for i in range(NT)], sem("s_y"), sem("s_out")

        block = ctx.enter_context(nc.Block())

        def x_dram(lt):
            return x_sample[0, lt * P:(lt + 1) * P, :] if lt < NS else x_prompt[0]

        def w_source(b):
            kind, i = b
            col = {"ada": 0, "u": 0, "q": 512, "k": 1024, "v": 1536, "g": 2560, "sr": D, "ro": 0, "sp": 0, "wo": 0}
            mat = {"ada": w_ada, "sr": w_branch_gate, "sp": w_branch_gate, "ro": w_ret_out, "wo": w_out}
            if kind == "po":
                return w_pool_out[0, :, i * 512:(i + 1) * 512].rearrange("(k p) f -> p k f", p=P), 512
            m = mat.get(kind, w_in)
            o = col[kind] + 256 * i
            return m[0, :, o:o + 256].rearrange("(k p) f -> p k f", p=P), 256

        def wait_raw_free(eng, n):
            if n >= RAW_T:
                b = BLOCKS[n - RAW_T]
                if b[0] == "ada":
                    eng.wait_ge(ada_done, b[1] + 1)
                else:
                    eng.wait_ge(w_lo_done, SPLIT_AT[b] + 1)

        def e_block(n):
            if n < 2 * NJ:
                return (w_exp_gate, w_exp_up)[n % 2], n // 2
            return w_exp_down, n - 2 * NJ

        @block.sync
        def _(sp):
            sp.dma_start(ident[:], tables[:, C_ID:C_ID + P]).then_inc(s_cond, 16)
            row = 0
            for v in (c[0], c_ctx, norm1_g[0], norm2_g[0], ret_gn_g[0], pool_scale[0], b_branch_gate[0], b_ada[0]):
                n = v.shape[0] // P
                sp.dma_start(vec_rows[row:row + n, :], v.rearrange("(k p) -> k p", p=P)).then_inc(s_cond, 16)
                row += n
            assert row == N_VEC
            for n, b in enumerate(BLOCKS):
                wait_raw_free(sp, n)
                src, width = w_source(b)
                sp.dma_start(raw_t[:, n % RAW_T, :].rearrange("p (k f) -> p k f", f=width), src)\
                  .then_inc(w_landed[n % RAW_T], 16)
            with sp.Fori(0, NE) as e:
                for n in range(NB):
                    sp.wait_ge(e_lo, e * NB + n + 1)
                    m, j = e_block(n)
                    slot = raw_e[:, n % RAW_E, :]
                    if n < 2 * NJ:
                        src = m[0, bass.ds(e, 1), :, j * FB:(j + 1) * FB].rearrange("a (k p) f -> p (a k) f", p=P)
                        dst = slot.rearrange("p (k f) -> p k f", f=FB)
                    else:
                        q, part = j // 2, j % 2
                        src = m[0, bass.ds(e, 1), part * FTH * P:(part + 1) * FTH * P, q * DQ:(q + 1) * DQ]\
                            .rearrange("a (k p) f -> p (a k) f", p=P)
                        dst = slot.rearrange("p (k f) -> p k f", f=DQ)
                    sp.dma_start(dst, src).then_inc(e_landed[n % RAW_E], 16)
            sp.wait_ge(s_acc, 16 * NT + 16 * NE)
            for lt in range(NT):
                sp.dma_start(y_tile[:, lt, :], acc_dram[lt * P:(lt + 1) * P, :]).then_inc(s_fin[lt], 16)
            for lt in range(NT):
                sp.wait_ge(s_y, lt + 1)
                dst = y_sample[0, lt * P:(lt + 1) * P, :] if lt < NS else y_prompt[0]
                sp.dma_start(dst, y_tile[:, lt, :]).then_inc(s_out, 16)
            sp.wait_ge(s_out, 16 * NT)
            sp.wait_ge(s_stdma, 16 * 2 * H)

        @block.gpsimd
        def _(pool):
            for lt in range(NT):
                pool.dma_start(x_in[:, lt, :], x_dram(lt)).then_inc(s_x[lt], 16)
            n_const = 0
            for dst, src in (
                (cos_t[:].rearrange("p a b -> p (a b)"), tables[:, C_COS:C_COS + 512]),
                (sin_t[:].rearrange("p a b -> p (a b)"), tables[:, C_SIN:C_SIN + 512]),
                (kpow[:], tables[:, C_KP:C_KP + 2]), (edge[:].rearrange("p a b -> p (a b)"), tables[:, C_EDGE:C_END]),
                (wr_sb[:], w_router[0].rearrange("(k p) e -> p k e", p=P)),
                (wp_sb[:], w_pool[0].rearrange("g c d -> c g d")),
            ):
                pool.dma_start(dst, src).then_inc(s_const, 16)
                n_const += 1
            assert n_const == N_CONST
            pool.dma_start(lgam[:].rearrange("p a b -> p (a b)"),
                           ret_decay[0:1].rearrange("a d h -> a (d h)").to_broadcast([P, 2 * H])).then_inc(s_decay, 16)
            pool.dma_start(pows[:].rearrange("p a b -> p (a b)"), tables[:, C_DPL:C_DPL + 512]).then_inc(s_pow, 16)
            pool.wait_ge(s_tab, 10)
            for h in range(H):
                if h >= 2:
                    pool.wait_ge(acc_full, ACC.full(("o", h - 2, 4)))
                    pool.wait_ge(s_state, 6 * (h - 1))
                for d in range(2):
                    pool.dma_start(s0[:, h % 2, d, :], state_ret[0, 0, d, h]).then_inc(s_s0[h % 2], 16)
                if h == 0:
                    pool.wait_ge(s_rope, 4 * NT)
                else:
                    pool.wait_ge(acc_full, ACC.full(("kvb", h - 1, 4)))
                ks = k_n[:, :, h * DK:(h + 1) * DK]
                nc.gpsimd.tensor_scalar(kf[:], ks, kdec[:, 0, h:h + 1], None, ALU.mult).then_inc(s_kdec, 1)
                nc.gpsimd.tensor_scalar(kb[:], ks, kdec[:, 1, h:h + 1], None, ALU.mult).then_inc(s_kdec, 1)
                if h == 0:
                    pool.wait_ge(tr_read["act"], 4 * NT + 1)
                else:
                    pool.wait_ge(acc_full, ACC.full(("o", h - 1, 4)))
                qs = q_t[:, h, 0:L_S].rearrange("p (a b) -> p a b", a=NS)
                for dst, tab in ((qf, qfp), (qb, qbp)):
                    nc.gpsimd.tensor_tensor(dst[:], qs, tab[:, h, :].unsqueeze(1).to_broadcast([P, NS, P]),
                                            ALU.mult).then_inc(s_qdec, 1)
                pool.wait_ge(acc_read["dve"], DVE_READ["kvb", h, 4])
                for d in range(2):
                    pool.dma_start(new_state[0, 0, d, h], qk_raw[:, d, :]).then_inc(s_stdma, 16)
            pool.wait_ge(s_adar, 1)
            pool.dma_start(ada_dram, adar[:]).then_inc(s_adaw, 16)
            pool.wait_ge(s_adaw, 16)

            def ada_row(param, cond_i):
                return ada_dram.rearrange("(j s) p -> s j p", s=2)[cond_i:cond_i + 1, 8 * param:8 * param + 8, :]

            for cnd in range(2):
                pool.dma_start(g1_b[:, cnd, :].rearrange("p (j q) -> p j q", j=8),
                               ada_row(2, cnd).to_broadcast([P, 8, P])).then_inc(s_bc, 16)
                pool.dma_start(gs2_b[:, cnd, :].rearrange("p (j q) -> p j q", j=8),
                               ada_row(4, cnd).to_broadcast([P, 8, P])).then_inc(s_bc, 16)
            steps = 0
            pad = 8
            for g, w in enumerate(WINDOWS):
                pool.wait_ge(acc_read["act"], ACT_READ_U[g])
                for lo, n in ((0, L_S), (L_S, L_P)):
                    if g or lo:
                        pool.wait_ge(s_pool, steps)
                    for i in range(2):
                        nc.gpsimd.memset(pool_a[:, i, :], 0.0).then_inc(s_pool, 1)
                    steps += 2
                    pool.wait_ge(s_pool, steps)
                    u = pooled[:, g, lo:lo + n]
                    nc.gpsimd.tensor_copy(pool_a[:, 0, pad:pad + n], u).then_inc(s_pool, 1)
                    steps += 1
                    cur, span = 0, 1
                    while span < w:
                        pool.wait_ge(s_pool, steps)
                        m = n + 2 * pad - 2 * span + 1
                        nc.gpsimd.tensor_tensor(pool_a[:, 1 - cur, 0:m], pool_a[:, cur, 0:m],
                                                pool_a[:, cur, span:span + m], ALU.add).then_inc(s_pool, 1)
                        steps += 1
                        cur, span = 1 - cur, 2 * span
                    o = pad - w // 2
                    pool.wait_ge(s_pool, steps)
                    nc.gpsimd.tensor_tensor(pool_a[:, cur, o:o + 8], pool_a[:, cur, o:o + 8], edge[:, g, 0:8],
                                            ALU.mult).then_inc(s_pool, 1)
                    nc.gpsimd.tensor_tensor(pool_a[:, cur, o + n - 8:o + n], pool_a[:, cur, o + n - 8:o + n],
                                            edge[:, g, 8:16], ALU.mult).then_inc(s_pool, 1)
                    steps += 2
                    pool.wait_ge(s_pool, steps)
                    nc.gpsimd.tensor_scalar(pool_a[:, cur, o:o + n], pool_a[:, cur, o:o + n], 1.0 / w, None,
                                            ALU.mult).then_inc(s_pool, 1)
                    steps += 1
                    pool.wait_ge(s_pool, steps)
                    nc.gpsimd.tensor_tensor(u, pool_a[:, cur, o:o + n], u, ALU.subtract).then_inc(s_pool, 1)
                    steps += 1
            pool.wait_ge(s_pool, steps)
            nc.gpsimd.memset(pool_a[:, 0, 0:1], 0.0).then_inc(s_pooled, 1)
            pool.wait_ge(s_mixfree, 1)
            for lt in range(NT):
                pool.dma_start(x2[:, lt, :], x_dram(lt)).then_inc(s_x2in[lt], 16)
            pool.wait_ge(acc_full, ACC.n)
            for cnd in range(2):
                pool.dma_start(sh2_b[:, cnd, :].rearrange("p (j q) -> p j q", j=8),
                               ada_row(3, cnd).to_broadcast([P, 8, P])).then_inc(s_bc, 16)
            for lt in range(NT):
                pool.wait_ge(s_h2, lt + 1)
                pool.dma_start(acc_dram[lt * P:(lt + 1) * P, :], x2[:, lt, :]).then_inc(s_acc, 16)
                pool.dma_start(h2_dram[lt * P:(lt + 1) * P, :], h2[:, lt % 2, :]).then_inc(s_h2w[lt], 16)
            pool.wait_ge(s_acc, 16 * NT)
            for lt in range(NT):
                pool.wait_ge(s_h2w[lt], 16)
            pool.dma_start(fg_b[:], final_norm_g.rearrange("(a n) -> a n", a=1).to_broadcast([P, D])).then_inc(s_fg, 16)
            for cnd, lo, n in ((0, 0, C_S), (1, C_S, C_P)):
                pool.dma_start(g2_rows[lo:lo + n, :].rearrange("p (j q) -> p j q", j=8),
                               ada_row(5, cnd).to_broadcast([n, 8, P])).then_inc(s_g2, 16)

            def hold():
                nc.gpsimd.tensor_tensor(small[:, 62:64], kpow[:], kpow[:], ALU.add).then_inc(s_hold, 1)

            def gather():
                pool.indirect_dma_start(x_rows[:], None, h2_dram, bass.IndirectOffsetOnAxis(idx_gather[:, 0:1], 0))\
                    .then_inc(e_gath, 16)

            def scatter():
                pool.indirect_dma_start(acc_dram, bass.IndirectOffsetOnAxis(idx_scatter[:, 0:1], 0), out_rows[:], None,
                                        compute_op=ALU.add).then_inc(s_acc, 16)

            pool.wait_ge(e_idx, 1)
            hold()
            gather()

            def expert(e, last):
                if not last:
                    pool.wait_ge(e_idx, 2 * e + 2)
                    pool.wait_ge(e_tr, NG * e + NG)
                    pool.wait_ge(s_hold, 2 * e + 1)
                    hold()
                    gather()
                pool.wait_ge(e_idx, 2 * e + 3 if not last else 2 * e + 2)
                pool.wait_ge(e_out, NQ * e + 2 * NQ)
                pool.wait_ge(s_hold, 2 * e + 2 if not last else 2 * e + 1)
                hold()
                scatter()

            with pool.Fori(0, NE - 1) as e:
                expert(e, False)
            expert(NE - 1, True)

        def qk_t(s, tr):
            kind, i = SPLITS[s // NT]
            lt = s % NT
            src = tr(("t", kind, i, lt))
            dst = (q_t if kind == "q" else k_t)[:, 2 * i:2 * i + 2, lt * P:(lt + 1) * P]
            nc.scalar.activation(dst, src[:, 0:256].rearrange("p (a b) -> p a b", a=2), ACT.Copy)\
              .then_inc(tr_read["act"], 1)

        def on_t(h, tr):
            for lt in range(NT):
                src = tr(("on", h, lt))
                nc.scalar.activation(o_t[:, 2 * h:2 * h + 2, lt * P:(lt + 1) * P],
                                     src[:, 0:256].rearrange("p (a b) -> p a b", a=2), ACT.Copy)\
                  .then_inc(tr_read["act"], 1)

        @block.scalar
        def _(act):
            steps = [0]

            def tick(ins):
                steps[0] += 1
                ins.then_inc(act_step, 1)
                act.wait_ge(act_step, steps[0])

            def split(m):
                if m >= len(SPLITS):
                    return
                n = INDEX[SPLITS[m]]
                act.wait_ge(w_landed[n % RAW_T], 16 * (n // RAW_T + 1))
                if m >= SPLIT_T:
                    act.wait_ge(acc_full, LAST_UNIT[SPLITS[m - SPLIT_T]])
                nc.scalar.activation(wt_hi[:, m % SPLIT_T, :], raw_t[:, n % RAW_T, :], ACT.Copy).then_inc(w_hi_done, 1)

            def acc(u):
                act.wait_ge(acc_full, ACC.full(u))
                return bank[ACC.bank(u)]

            def tr(u):
                act.wait_ge(tr_full, TR.full(u))
                return bank[TR.bank(u)]

            nc.scalar.activation(cols[:], tr(("vec", 0, 0))[:, 0:N_VEC], ACT.Copy).then_inc(tr_read["act"], 1)
            act.wait_ge(tr_read["act"], 1)
            nc.scalar.activation(scond[:], cols[:, 0:16].rearrange("p (a b) -> p a b", a=2), ACT.Silu).then_inc(s_scond, 1)
            act.wait_ge(s_decay, 16)
            nc.scalar.activation(lgam[:], lgam[:], ACT.Exp).then_inc(s_exp, 1)
            act.wait_ge(s_lgam, 1)
            act.wait_ge(s_pow, 16)
            for h in range(H):
                nc.scalar.activation(qfp[:, h, :], pows[:, 2, :], ACT.Exp, scale=lgam[:, 0, h:h + 1]).then_inc(s_tab, 1)
                nc.scalar.activation(qbp[:, h, :], pows[:, 3, :], ACT.Exp, scale=lgam[:, 1, h:h + 1]).then_inc(s_tab, 1)
            act.wait_ge(s_lgam, 3)
            nc.scalar.activation(kdec[:], kdec[:], ACT.Exp).then_inc(s_tab, 1)
            nc.scalar.activation(cdec[:], lgam[:], ACT.Exp, scale=float(P)).then_inc(s_tab, 1)
            act.wait_ge(s_marg, 2 * H)
            nc.scalar.activation(mask[:], mask[:], ACT.Exp).then_inc(s_tab, 1)
            for lt in range(NT):
                act.wait_ge(s_x[lt], 16)
                if lt:
                    act.wait_ge(s_ms, lt)
                nc.scalar.activation(x_sq[:], x_in[:, lt, :], ACT.Square, accum_out=small[:, lt:lt + 1]).then_inc(s_ms, 1)
            act.wait_ge(s_rstd, 1)
            nc.scalar.activation(small[:, 16:21], small[:, 8:13], ACT.Sqrt).then_inc(s_sqrt, 1)
            act.wait_ge(s_rstd, 2)
            def normalise(lt):
                if lt >= 2:
                    act.wait_ge(tr_full, TR.full(("h", lt - 2, 1)))
                nc.scalar.activation(xn[:, lt % 2, :], x_in[:, lt, :], ACT.Copy, scale=small[:, 24 + lt:25 + lt])\
                  .then_inc(s_xn, 1)

            normalise(0)
            normalise(1)
            for lt in range(NT):
                if lt == 1:
                    split(0)
                if lt >= 1 and lt + 1 < NT:
                    normalise(lt + 1)
                for i in range(2):
                    act.wait_ge(s_htmp, 4 * (2 * lt + i + 1))
                    nc.scalar.activation(act_hi[:, 4 * i:4 * i + 4, lt * P:(lt + 1) * P],
                                         h_tmp[:, i, :].rearrange("p (a b) -> p a b", a=4), ACT.Copy).then_inc(s_hhi, 1)
            for m in range(8):
                kind, i = SPLITS[m]
                if m < 7:
                    split(m + 1)
                for lt in range(NT):
                    u = (kind, i, lt)
                    src = acc(u)[:, 0:256]
                    if kind == "v":
                        nc.scalar.activation(v_n[:, lt, i * 256:(i + 1) * 256], src, ACT.Copy).then_inc(acc_read["act"], 1)
                        continue
                    s = m * NT + lt
                    if s >= 2:
                        act.wait_ge(s_rope, s - 1)
                    nc.scalar.activation(qk_raw[:, s % 2, :], src, ACT.Copy,
                                         scale=1.0 if kind == "q" else DK ** -0.5).then_inc(acc_read["act"], 1)
                    if s >= 1:
                        qk_t(s - 1, tr)
                if m == 3:
                    qk_t(4 * NT - 1, tr)
            for h in range(H):
                if h:
                    on_t(h - 1, tr)
                for lt in range(NT):
                    src = acc(("o", h, lt))[:, 0:DV]
                    if lt == 0 and h:
                        act.wait_ge(tr_full, TR.full(("on", h - 1, NT - 1)))
                    nc.scalar.activation(o_raw[:, lt, :], src, ACT.Copy).then_inc(acc_read["act"], 1)
                act.wait_ge(s_mv, h + 1)
                nc.scalar.activation(small[:, 40:45], small[:, 32:37], ACT.Sqrt).then_inc(s_osq, 1)
            src = tr(("ada", 0, 0))
            nc.scalar.activation(adar[:], src[0:96, 0:P], ACT.Copy).then_inc(tr_read["act"], 1)
            act.wait_ge(tr_read["act"], TR_ACT["ada", 0, 0])
            nc.scalar.activation(small[:, 60:61], small[:, 24:25], ACT.Copy).then_inc(s_adar, 1)
            act.wait_ge(s_stdma, 16 * 2 * H)
            split(8)
            q = 0
            for m in range(8, 28):
                kind, i = SPLITS[m]
                if kind == "wo":
                    break
                if kind == "sp" and i == 0:
                    for z in range(8):
                        act.wait_ge(s_gmul, 16 + z + 1)
                        g, f = z // 2, z % 2
                        nc.scalar.activation(py_hi[:, g, f * HALF:(f + 1) * HALF], rtmp[:, z % 2, :], ACT.Copy)\
                          .then_inc(s_ghi, 1)
                split(m + 1)
                if kind == "g" and i == 1:
                    on_t(H - 1, tr)
                for cc in range(4 if kind == "po" else 2):
                    for f in range(2):
                        span = slice(f * HALF, (f + 1) * HALF)
                        if kind == "g":
                            ct = 2 * i + cc
                            src = acc((kind, i, cc, f))[:, 0:HALF]
                            if q >= 2:
                                act.wait_ge(s_gmul, q - 1)
                            nc.scalar.activation(gtmp[:, q % 2, :], src, ACT.Silu).then_inc(acc_read["act"], 1)
                            act.wait_ge(s_gmul, q + 1)
                            nc.scalar.activation(ret_hi[:, ct, span], rtmp[:, q % 2, :], ACT.Copy).then_inc(s_ghi, 1)
                            q += 1
                        elif kind == "u":
                            ct = 2 * i + cc
                            src = acc((kind, i, cc, f))[:, 0:HALF]
                            nc.scalar.activation(pooled[:, ct, span], src, ACT.Copy).then_inc(acc_read["act"], 1)
                        elif kind in ("sr", "sp"):
                            ct = 2 * i + cc
                            src = acc((kind, i, cc, f))[:, 0:HALF]
                            if kind == "sr" and ct == 0:
                                act.wait_ge(s_gmul, 16)
                            dst, b0 = (mix, 8) if kind == "sr" else (sig_p, 0)
                            nc.scalar.activation(dst[:, ct, span], src, ACT.Sigmoid, bias=bbg[:, b0 + ct:b0 + ct + 1])\
                              .then_inc(acc_read["act"], 1)
                        elif kind == "po":
                            ct = 4 * i + cc
                            z = 2 * ct + f
                            act.wait_ge(s_gmul, 24 + z + 1)
                            nc.scalar.activation(act_hi[:, ct, span], rtmp[:, z % 2, :], ACT.Copy).then_inc(s_ghi, 1)
            for m in range(28, 32):
                split(m + 1)
            for lt in range(NT):
                act.wait_ge(s_x2, 3 * NT + lt + 1)
                if lt:
                    act.wait_ge(act_step, steps[0])
                tick(nc.scalar.activation(x2_sq[:], x2[:, lt, :], ACT.Square, accum_out=small[:, lt:lt + 1]))
                act.wait_ge(s_rstd, 3 + 2 * lt)
                nc.scalar.activation(small[:, 8 + lt:9 + lt], small[:, 16 + lt:17 + lt], ACT.Sqrt).then_inc(s_sqrt, 1)
                for i in range(2):
                    if lt >= 2 and i == 0:
                        act.wait_ge(tr_full, TR.full(("lg", lt - 2, 0)))
                    src = tr(("h2", lt, i))
                    nc.scalar.activation(h2_t[:, lt % 2, i * 512:(i + 1) * 512], src[:, :], ACT.Copy)\
                      .then_inc(tr_read["act"], 1)
                act.wait_ge(s_rmax, lt + 1)
                if lt >= 2:
                    act.wait_ge(s_aff, lt - 1)
                nc.scalar.activation(aff[:, lt % 2, :], aff[:, lt % 2, :], ACT.Exp, bias=small[:, 48:49],
                                     accum_out=small[:, 50:51]).then_inc(s_rexp, 1)
                src = tr(("af", lt, 0))
                nc.scalar.activation(aff_t[:, 0, lt * P:(lt + 1) * P], src[0:NE, 0:P], ACT.Copy)\
                  .then_inc(tr_read["act"], 1)
            def e_split(e, n):
                act.wait_ge(e_landed[n % RAW_E], (e * (NB // RAW_E) + n // RAW_E + 1) * 16)
                act.wait_ge(e_used, e * NB + n + 1)
                nc.scalar.activation(we_hi[:, n % SPLIT_E, :], raw_e[:, n % RAW_E, :], ACT.Copy).then_inc(e_hi, 1)

            def tr_hi(e, g):
                act.wait_ge(e_tr, NG * (e + 1) + g + 1)
                dst, n = (xs_hi, 4) if g >= NJ else (hd_hi, TILE_EDGE[g % 4 + 1] - TILE_EDGE[g % 4])
                t0 = 4 * (g - NJ) if g >= NJ else FTH * (g // 4) + TILE_EDGE[g % 4]
                nc.scalar.activation(dst[:, t0:t0 + n, :], bank[5 + g % 2][:, 0:n * CAP].rearrange("p (a b) -> p a b", a=n),
                                     ACT.Copy).then_inc(e_tr_hi, 1 if not (isinstance(e, int) and e < 0 and g == NJ) else NJ + 1)

            e_split(0, 0)
            tr_hi(-1, NJ)
            tr_hi(-1, NJ + 1)
            act.wait_ge(s_idx, 2)
            nc.scalar.activation(small[:, 61:62], small[:, 24:25], ACT.Copy).then_inc(e_silu, NJ)

            def expert(e, last):
                for n in range(NB):
                    if n + 1 < NB:
                        e_split(e, n + 1)
                    elif not last:
                        e_split(e + 1, 0)
                    j = n // 2
                    if n < 2 * NJ and n % 2 == 0:
                        act.wait_ge(e_used, e * NB + n + 1 + SPLIT_E)
                        act.wait_ge(e_hid, NJ * e + NJ + j - 1)
                        nc.scalar.activation(silu_g[:, j % 2, :], bank[j % 2][0:CAP, 0:FB], ACT.Silu).then_inc(e_silu, 1)
                    if n in TR_AFTER:
                        g = TR_AFTER[n]
                        if g < NJ or not last:
                            tr_hi(e, g)

            with act.Fori(0, NE - 1) as e:
                expert(e, False)
            expert(NE - 1, True)
            for lt in range(NT):
                act.wait_ge(s_fin[lt], 16)
                tick(nc.scalar.activation(y_sq[:], y_tile[:, lt, :], ACT.Square, accum_out=small[:, lt:lt + 1]))
            act.wait_ge(s_rstd, 3 + 2 * NT)
            nc.scalar.activation(small[:, 16:21], small[:, 8:13], ACT.Sqrt).then_inc(s_sqrt, 1)

        @block.vector
        def _(dve):
            steps = [0]

            def tick(ins):
                steps[0] += 1
                ins.then_inc(dve_step, 1)
                dve.wait_ge(dve_step, steps[0])

            def split(m):
                if m >= len(SPLITS):
                    return
                n = INDEX[SPLITS[m]]
                dve.wait_ge(w_hi_done, m + 1)
                nc.vector.tensor_tensor(wt_lo[:, m % SPLIT_T, :], raw_t[:, n % RAW_T, :],
                                        wt_hi[:, m % SPLIT_T, :].bitcast(F32), ALU.subtract).then_inc(w_lo_done, 1)

            def acc(u):
                dve.wait_ge(acc_full, ACC.full(u))
                return bank[ACC.bank(u)]

            def tr(u):
                dve.wait_ge(tr_full, TR.full(u))
                return bank[TR.bank(u)]

            dve.wait_ge(s_exp, 1)
            dve.wait_ge(tr_read["act"], 1)
            dve.wait_ge(s_const, 16 * N_CONST)
            nc.vector.tensor_scalar(lgam[:], lgam[:], -1.0, None, ALU.mult).then_inc(s_lgam, 1)
            dve.wait_ge(s_lgam, 1)
            dve.wait_ge(s_pow, 16)
            for d in range(2):
                nc.vector.tensor_scalar(kdec[:, d, :], lgam[:, d, :], kpow[:, d:d + 1], None, ALU.mult).then_inc(s_lgam, 1)
            for h in range(H):
                nc.vector.tensor_scalar(mask[:, h, :], pows[:, 0, :], lgam[:, 0, h:h + 1], None, ALU.mult).then_inc(s_marg, 1)
            dve.wait_ge(s_marg, H)
            for h in range(H):
                nc.vector.scalar_tensor_tensor(out=mask[:, h, :], in0=pows[:, 1, :], scalar=lgam[:, 1, h:h + 1],
                                               in1=mask[:, h, :], op0=ALU.mult, op1=ALU.add).then_inc(s_marg, 1)
            dve.wait_ge(s_ms, NT)
            nc.vector.tensor_scalar(small[:, 8:13], small[:, 0:NT], 1.0 / D, EPS, ALU.mult, ALU.add).then_inc(s_rstd, 1)
            dve.wait_ge(s_sqrt, 1)
            nc.vector.reciprocal(small[:, 24:29], small[:, 16:21]).then_inc(s_rstd, 1)
            dve.wait_ge(ada_done, 8)
            nc.vector.tensor_tensor(ada_t[:, 0:16, :], ada_ps[:, 0:32].rearrange("p (a b) -> p a b", b=2),
                                    bada[:, 0:16].unsqueeze(2).to_broadcast([P, 16, 2]), ALU.add).then_inc(s_ada0, 1)
            dve.wait_ge(s_ada0, 1)
            nc.vector.scalar_tensor_tensor(out=gs1[:], in0=ada_t[:, 8:16, :], scalar=1.0,
                                           in1=n1g.unsqueeze(2).to_broadcast([P, KT, 2]), op0=ALU.add, op1=ALU.mult)\
              .then_inc(s_gs, 1)
            dve.wait_ge(s_gs, 1)
            for lt in range(NT):
                cnd = int(lt == NS)
                if lt == 1:
                    split(0)
                for i in range(2):
                    src = tr(("h", lt, i))
                    if lt:
                        dve.wait_ge(s_hlo, 2 * (lt - 1) + i + 1)
                    for a in range(4):
                        k = 4 * i + a
                        ins = nc.vector.tensor_scalar(h_tmp[:, i, a * P:(a + 1) * P], src[:, a * P:(a + 1) * P],
                                                      gs1[:, k, cnd:cnd + 1], ada_t[:, k, cnd:cnd + 1], ALU.mult, ALU.add)
                        ins.then_inc(s_htmp, 1)
                    dve.wait_ge(s_htmp, 4 * (2 * lt + i + 1))
                    dve.wait_ge(s_hhi, 2 * lt + i + 1)
                    sl = slice(lt * P, (lt + 1) * P)
                    nc.vector.tensor_tensor(act_lo[:, 4 * i:4 * i + 4, sl], h_tmp[:, i, :].rearrange("p (a b) -> p a b", a=4),
                                            act_hi[:, 4 * i:4 * i + 4, sl].bitcast(F32), ALU.subtract).then_inc(s_hlo, 1)
            for m in range(8):
                kind, i = SPLITS[m]
                if m < 7:
                    split(m + 1)
                if kind == "v":
                    continue
                for lt in range(NT):
                    s = m * NT + lt
                    dve.wait_ge(acc_read["act"], s + 1)
                    if kind == "q":
                        if s >= 2:
                            dve.wait_ge(tr_full, TR.full(("t",) + SPLITS[(s - 2) // NT] + ((s - 2) % NT,)))
                        dst = q_rope[:, s % 2, :]
                    else:
                        dst = k_n[:, lt, i * 256:(i + 1) * 256]
                    raw = qk_raw[:, s % 2, :]
                    if lt == NS:
                        nc.vector.tensor_copy(dst, raw).then_inc(s_rope, 1)
                        continue
                    d2 = dst.rearrange("p (h d) -> p h d", h=2)
                    d4 = dst.rearrange("p (h d e) -> p h d e", h=2, e=2)
                    r2 = raw.rearrange("p (h d) -> p h d", h=2)
                    r4 = raw.rearrange("p (h d e) -> p h d e", h=2, e=2)
                    s4 = sin_t[:, lt, :].rearrange("p (d e) -> p d e", e=2)
                    tmp = rope_tmp[:, 0:256].rearrange("p (h d e) -> p h d e", h=2, e=2)
                    nc.vector.tensor_tensor(d2, r2, cos_t[:, lt, :].unsqueeze(1).to_broadcast([P, 2, DK]), ALU.mult)\
                      .then_inc(dve_step, 1)
                    nc.vector.tensor_tensor(tmp[:, :, :, 0], r4[:, :, :, 1], s4[:, :, 0].unsqueeze(1).to_broadcast([P, 2, 64]),
                                            ALU.mult).then_inc(dve_step, 1)
                    nc.vector.tensor_tensor(tmp[:, :, :, 1], r4[:, :, :, 0], s4[:, :, 1].unsqueeze(1).to_broadcast([P, 2, 64]),
                                            ALU.mult).then_inc(dve_step, 1)
                    steps[0] += 3
                    dve.wait_ge(dve_step, steps[0])
                    nc.vector.tensor_tensor(dst, dst, rope_tmp[:, 0:256], ALU.add).then_inc(s_rope, 1)
                    dve.wait_ge(s_rope, s + 1)
            dve.wait_ge(s_tab, 11)
            n_probs = 0
            for h in range(H):
                n_state = 6 * h
                for u in [("kvf", h, lt) for lt in (0, 1, 2)] + [("kvb", h, lt) for lt in (3, 2, 1)]:
                    d = int(u[0] == "kvb")
                    i = 3 - u[2] if d else u[2]
                    if i == 0:
                        dve.wait_ge(s_s0[h % 2], 32 * (h // 2 + 1))
                        before = s0[:, h % 2, d, :]
                    else:
                        dve.wait_ge(s_state, n_state)
                        before = states[:, 3 * d + i - 1, :]
                    src = acc(u)[:, 0:DV]
                    nc.vector.scalar_tensor_tensor(out=states[:, 3 * d + i, :], in0=before, scalar=cdec[:, d, h:h + 1],
                                                   in1=src, op0=ALU.mult, op1=ALU.add).then_inc(s_state, 1)
                    n_state += 1
                for d, name in ((0, "kvf"), (1, "kvb")):
                    if h:
                        dve.wait_ge(s_stdma, 16 * (2 * h))
                    src = acc((name, h, 4))[:, 0:DV]
                    nc.vector.tensor_copy(qk_raw[:, d, :], src).then_inc(acc_read["dve"], 1)
                for lt in range(NT):
                    src = acc(("sc", h, lt))[:, 0:P]
                    if n_probs >= 2:
                        ph, pl = divmod(n_probs - 2, NT)
                        dve.wait_ge(acc_full, ACC.full(("o", ph, pl)))
                    nc.vector.tensor_tensor(probs[:, n_probs % 2, :], src, mask[:, h, :], ALU.mult)\
                      .then_inc(acc_read["dve"], 1)
                    n_probs += 1
                for lt in range(NT):
                    dve.wait_ge(acc_read["act"], ACT_READ_O[h, lt])
                    tick(nc.vector.bn_stats(small[:, 52:58], o_raw[:, lt, :]))
                    tick(nc.vector.bn_aggr(mv[:, lt, :], small[:, 52:58]))
                nc.vector.tensor_scalar(small[:, 32:37], mv[:, :, 1], EPS, None, ALU.add).then_inc(s_mv, 1)
                dve.wait_ge(s_osq, h + 1)
                tick(nc.vector.reciprocal(small[:, 24:29], small[:, 40:45]))
                for lt in range(NT):
                    nc.vector.tensor_scalar(o_raw[:, lt, :], o_raw[:, lt, :], mv[:, lt, 0:1], small[:, 24 + lt:25 + lt],
                                            ALU.subtract, ALU.mult).then_inc(s_on, 1)
            dve.wait_ge(ada_done, 24)
            tick(nc.vector.tensor_tensor(ada_t[:, 16:48, :], ada_ps[:, 32:96].rearrange("p (a b) -> p a b", b=2),
                                         bada[:, 16:48].unsqueeze(2).to_broadcast([P, 32, 2]), ALU.add))
            nc.vector.scalar_tensor_tensor(out=ada_t[:, 32:40, :], in0=ada_t[:, 32:40, :], scalar=1.0,
                                           in1=n2g.unsqueeze(2).to_broadcast([P, KT, 2]), op0=ALU.add, op1=ALU.mult)\
              .then_inc(s_ada, 1)
            split(8)
            z = 0
            for m in range(8, 28):
                kind, i = SPLITS[m]
                if kind == "sp" and i == 0:
                    for g in range(4):
                        for f in range(2):
                            span = slice(f * HALF, (f + 1) * HALF)
                            src = acc(("pg", g, f))[:, 0:HALF]
                            if z >= 2:
                                dve.wait_ge(s_glo, z - 1)
                            nc.vector.tensor_scalar(rtmp[:, z % 2, :], src, pscale[:, g:g + 1], None, ALU.mult)\
                              .then_inc(s_gmul, 1)
                            dve.wait_ge(s_ghi, z + 1)
                            nc.vector.tensor_tensor(py_lo[:, g, span], rtmp[:, z % 2, :],
                                                    py_hi[:, g, span].bitcast(F32), ALU.subtract).then_inc(s_glo, 1)
                            z += 1
                split(m + 1)
                for cc in range(4 if kind == "po" else 2):
                    for f in range(2):
                        span = slice(f * HALF, (f + 1) * HALF)
                        if kind == "g":
                            ct = 2 * i + cc
                            dve.wait_ge(acc_read["act"], ACT_READ_G[z])
                            dve.wait_ge(tr_read["act"], TR_READ_ON[i])
                            if z >= 2:
                                dve.wait_ge(s_glo, z - 1)
                            nc.vector.scalar_tensor_tensor(out=rtmp[:, z % 2, :], in0=o_t[:, ct, span],
                                                           scalar=gng[:, ct:ct + 1], in1=gtmp[:, z % 2, :],
                                                           op0=ALU.mult, op1=ALU.mult).then_inc(s_gmul, 1)
                            dve.wait_ge(s_ghi, z + 1)
                            nc.vector.tensor_tensor(ret_lo[:, ct, span], rtmp[:, z % 2, :],
                                                    ret_hi[:, ct, span].bitcast(F32), ALU.subtract).then_inc(s_glo, 1)
                            z += 1
                        elif kind == "ro":
                            ct = 2 * i + cc
                            src = acc((kind, i, cc, f))[:, 0:HALF]
                            dve.wait_ge(acc_read["act"], ACT_READ_SR)
                            nc.vector.tensor_tensor(mix[:, ct, span], src, mix[:, ct, span], ALU.mult)\
                              .then_inc(acc_read["dve"], 1)
                        elif kind == "po":
                            ct = 4 * i + cc
                            src = acc((kind, i, cc, f))[:, 0:HALF]
                            if z >= 2:
                                dve.wait_ge(s_glo, z - 1)
                            dve.wait_ge(acc_read["act"], ACT_READ_SP)
                            if ct == 0 and f == 0:
                                dve.wait_ge(acc_read["dve"], DVE_READ_RO)
                            nc.vector.tensor_tensor(rtmp[:, z % 2, :], src, sig_p[:, ct, span], ALU.mult)\
                              .then_inc(acc_read["dve"], 1)
                            dve.wait_ge(acc_read["dve"], DVE_READ[kind, i, cc, f])
                            nc.vector.tensor_tensor(rtmp[:, z % 2, :], rtmp[:, z % 2, :], mix[:, ct, span], ALU.add)\
                              .then_inc(s_gmul, 1)
                            dve.wait_ge(s_ghi, z + 1)
                            nc.vector.tensor_tensor(act_lo[:, ct, span], rtmp[:, z % 2, :],
                                                    act_hi[:, ct, span].bitcast(F32), ALU.subtract).then_inc(s_glo, 1)
                            z += 1
            dve.wait_ge(s_glo, z)
            nc.vector.tensor_copy(small[:, 61:62], kpow[:, 0:1]).then_inc(s_mixfree, 1)
            nc.vector.tensor_copy(small[:, 59:60], kpow[:, 0:1]).then_inc(e_lo, RAW_E)
            dve.wait_ge(s_bc, 64)
            for i in range(4):
                split(28 + i + 1)
                for lt in range(NT):
                    cnd = int(lt == NS)
                    cs = slice(i * 256, (i + 1) * 256)
                    src = acc(("wo", i, lt))[:, 0:256]
                    if i == 0:
                        dve.wait_ge(s_x2in[lt], 16)
                    tmp = rtmp[:, (NT * i + lt) % 2, 0:256]
                    if NT * i + lt >= 2:
                        dve.wait_ge(s_x2, NT * i + lt - 1)
                    nc.vector.tensor_tensor(tmp, src, g1_b[:, cnd, cs], ALU.mult).then_inc(acc_read["dve"], 1)
                    dve.wait_ge(acc_read["dve"], DVE_READ["wo", i, lt])
                    nc.vector.tensor_tensor(x2[:, lt, cs], x2[:, lt, cs], tmp, ALU.add).then_inc(s_x2, 1)
            dve.wait_ge(s_bc, 96)
            dve.wait_ge(s_x2, 4 * NT)
            for lt in range(NT):
                cnd = int(lt == NS)
                dve.wait_ge(act_step, lt + 1)
                nc.vector.tensor_scalar(small[:, 16 + lt:17 + lt], small[:, lt:lt + 1], 1.0 / D, EPS, ALU.mult, ALU.add)\
                  .then_inc(s_rstd, 1)
                dve.wait_ge(s_sqrt, 2 + lt)
                nc.vector.reciprocal(small[:, 24 + lt:25 + lt], small[:, 8 + lt:9 + lt]).then_inc(s_rstd, 1)
                dve.wait_ge(s_rstd, 4 + 2 * lt)
                if lt >= 2:
                    dve.wait_ge(s_h2w[lt - 2], 16)
                    dve.wait_ge(tr_full, TR.full(("h2", lt - 2, 1)))
                tick(nc.vector.scalar_tensor_tensor(out=h2[:, lt % 2, :], in0=x2[:, lt, :], scalar=small[:, 24 + lt:25 + lt],
                                                    in1=gs2_b[:, cnd, :], op0=ALU.mult, op1=ALU.mult))
                nc.vector.tensor_tensor(h2[:, lt % 2, :], h2[:, lt % 2, :], sh2_b[:, cnd, :], ALU.add).then_inc(s_h2, 1)
                src = tr(("lg", lt, 0))[:, 0:NE]
                if lt >= 2:
                    dve.wait_ge(tr_full, TR.full(("af", lt - 2, 0)))
                tick(nc.vector.reduce_max(small[:, 49:50], src, AX.X))
                nc.vector.tensor_copy(aff[:, lt % 2, :], src).then_inc(tr_read["dve"], 1)
                nc.vector.tensor_scalar(small[:, 48:49], small[:, 49:50], -1.0, None, ALU.mult).then_inc(s_rmax, 1)
                dve.wait_ge(s_rexp, lt + 1)
                tick(nc.vector.reciprocal(small[:, 51:52], small[:, 50:51]))
                nc.vector.tensor_scalar(aff[:, lt % 2, :], aff[:, lt % 2, :], small[:, 51:52], None, ALU.mult)\
                  .then_inc(s_aff, 1)
            dve.wait_ge(tr_read["act"], TR_READ_AF)
            for lo, n, cap, c0 in ((0, L_S, C_S, 0), (L_S, L_P, C_P, C_S)):
                src = 0
                for r in range(cap // 8):
                    o = slice(c0 + 8 * r, c0 + 8 * r + 8)
                    cur = aff_t[:, src, lo:lo + n]
                    tick(nc.vector.max(top_v[:, o], cur))
                    nc.vector.max_index(top_i[:, o], top_v[:, o], cur).then_inc(s_top, 1)
                    if r + 1 < cap // 8:
                        tick(nc.vector.match_replace(out=aff_t[:, 1 - src, lo:lo + n], in_to_replace=top_v[:, o],
                                                     in_values=cur, imm_value=-1.0))
                        src = 1 - src
            dve.wait_ge(s_top, CAP // 8)
            tick(nc.vector.tensor_copy(top_f[:], top_i[:]))
            nc.vector.tensor_scalar(top_f[:, C_S:CAP], top_f[:, C_S:CAP], float(L_S), None, ALU.add).then_inc(s_top, 1)
            src = tr(("ix", 0, 0))
            nc.vector.tensor_copy(idx_all[:], src[0:CAP, 0:NE]).then_inc(s_idx, 1)
            dve.wait_ge(s_idx, 1)
            nc.vector.tensor_copy(idx_gather[:], idx_all[:, 0:1]).then_inc(e_idx, 1)
            src = tr(("ga", 0, 0))
            nc.vector.tensor_copy(gate_all[:], src[0:CAP, 0:NE]).then_inc(s_idx, 1)
            dve.wait_ge(s_idx, 2)

            def e_split(e, n):
                dve.wait_ge(e_hi, e * NB + n + 1)
                nc.vector.tensor_tensor(we_lo[:, n % SPLIT_E, :], raw_e[:, n % RAW_E, :],
                                        we_hi[:, n % SPLIT_E, :].bitcast(F32), ALU.subtract).then_inc(e_lo, 1)

            def tr_lo(e, g, inc=1):
                dve.wait_ge(e_tr_hi, NG * (e + 1) + g + 1)
                hi, lo, n = (xs_hi, xs_lo, 4) if g >= NJ else (hd_hi, hd_lo, TILE_EDGE[g % 4 + 1] - TILE_EDGE[g % 4])
                t0 = 4 * (g - NJ) if g >= NJ else FTH * (g // 4) + TILE_EDGE[g % 4]
                nc.vector.tensor_tensor(lo[:, t0:t0 + n, :], bank[5 + g % 2][:, 0:n * CAP].rearrange("p (a b) -> p a b", a=n),
                                        hi[:, t0:t0 + n, :].bitcast(F32), ALU.subtract).then_inc(e_tr_split, inc)

            e_split(0, 0)
            tr_lo(-1, NJ, NJ + 1)
            tr_lo(-1, NJ + 1)
            nc.vector.tensor_copy(small[:, 58:59], kpow[:, 0:1]).then_inc(e_hid, NJ)
            nc.vector.tensor_copy(small[:, 57:58], kpow[:, 0:1]).then_inc(e_out, NQ)
            dve.wait_ge(s_g2, 32)

            def expert(e, last):
                if not last:
                    dve.wait_ge(e_gath, 16 * e + 16)
                    nc.vector.tensor_copy(idx_gather[:], idx_all[:, bass.ds(e + 1, 1)]).then_inc(e_idx, 1)
                for n in range(NB):
                    if n + 1 < NB:
                        e_split(e, n + 1)
                    elif not last:
                        e_split(e + 1, 0)
                    j = n // 2
                    if n < 2 * NJ and n % 2:
                        dve.wait_ge(e_used, e * NB + n + 1 + SPLIT_E)
                        dve.wait_ge(e_silu, NJ * e + NJ + j + 1)
                        g = j - 3 - (j % 4 == 3)
                        dve.wait_ge(e_tr, NG * e + (NG + g + 1 if g >= 0 else NJ + g + 1))
                        nc.vector.tensor_tensor(hid[:, (j % 4) * FB:(j % 4 + 1) * FB], silu_g[:, j % 2, :],
                                                bank[2 + j % 2][0:CAP, 0:FB], ALU.mult).then_inc(e_hid, 1)
                    if n == 1:
                        dve.wait_ge(s_acc, 16 * NT + 16 * e)
                        col = slice(e, e + 1) if isinstance(e, int) else bass.ds(e, 1)
                        nc.vector.tensor_copy(idx_scatter[:], idx_all[:, col]).then_inc(e_idx, 1)
                        nc.vector.tensor_copy(gate_cur[:], gate_all[:, col]).then_inc(s_idx, 1)
                    if n in TR_AFTER:
                        g = TR_AFTER[n]
                        if g < NJ or not last:
                            tr_lo(e, g)
                    if n >= 2 * NJ and n % 2:
                        q = (n - 2 * NJ) // 2
                        dve.wait_ge(e_used, e * NB + n + 1 + SPLIT_E)
                        if q == 0:
                            dve.wait_ge(s_idx, e + 3)
                        nc.vector.scalar_tensor_tensor(
                            out=out_rows[:, q * DQ:(q + 1) * DQ], in0=bank[DOWN_BANK[q % 2]][0:CAP, 0:DQ],
                            scalar=gate_cur[:, 0:1], in1=g2_rows[:, q * DQ:(q + 1) * DQ],
                            op0=ALU.mult, op1=ALU.mult).then_inc(e_out, 1)

            with dve.Fori(0, NE - 1) as e:
                expert(e, False)
            expert(NE - 1, True)
            dve.wait_ge(s_fg, 16)
            dve.wait_ge(act_step, 2 * NT)
            nc.vector.tensor_scalar(small[:, 8:13], small[:, 0:NT], 1.0 / D, EPS, ALU.mult, ALU.add).then_inc(s_rstd, 1)
            dve.wait_ge(s_sqrt, 2 + NT)
            tick(nc.vector.reciprocal(small[:, 24:29], small[:, 16:21]))
            for lt in range(NT):
                nc.vector.scalar_tensor_tensor(out=y_tile[:, lt, :], in0=y_tile[:, lt, :], scalar=small[:, 24 + lt:25 + lt],
                                               in1=fg_b[:], op0=ALU.mult, op1=ALU.mult).then_inc(s_y, 1)

        @block.tensor
        def _(pe):
            mm = nc.tensor.matmul

            def acc(u):
                before = ACC.previous(u)
                if before:
                    pe.wait_ge(acc_read[before[0]], before[1])
                return bank[ACC.bank(u)]

            def tr(u):
                before = TR.previous(u)
                if before:
                    pe.wait_ge(tr_read[before[0]], before[1])
                return bank[TR.bank(u)]

            def transpose(dst, src):
                n = src.shape[0]
                return nc.tensor.transpose(dst, src, ident[0:n, 0:n])

            def ada(b):
                n = INDEX[("ada", b)]
                pe.wait_ge(w_landed[n % RAW_T], 16 * (n // RAW_T + 1))
                w = raw_t[:, n % RAW_T, :].rearrange("p (k f) -> p k f", k=KT)
                for j in range(2):
                    c0 = 2 * (2 * b + j)
                    for k in range(KT):
                        ins = mm(ada_ps[:, c0:c0 + 2], w[:, k, j * P:(j + 1) * P], scond[:, :, k], start=k == 0, stop=k == KT - 1)
                ins.then_inc(ada_done, 1)

            def three(out, pairs, count):
                i = 0
                for a, b in pairs:
                    ins = mm(out, a, b, start=i == 0, stop=i == count - 1)
                    i += 1
                return ins

            def by_tokens(b, hi, lo, after=None):
                m = SPLIT_AT[b]
                pe.wait_ge(w_lo_done, m + 1)
                wh = wt_hi[:, m % SPLIT_T, :].rearrange("p (k f) -> p k f", k=KT)
                wl = wt_lo[:, m % SPLIT_T, :].rearrange("p (k f) -> p k f", k=KT)
                for lt in range(NT):
                    if b == ("q", 0):
                        pe.wait_ge(s_hlo, 2 * lt + 2)
                    o = acc(b + (lt,))[:, 0:256]
                    sl = slice(lt * P, (lt + 1) * P)
                    pairs = [pr for k in range(KT) for pr in ((hi[:, k, sl], wh[:, k, :]), (lo[:, k, sl], wh[:, k, :]),
                                                               (hi[:, k, sl], wl[:, k, :]))]
                    three(o, pairs, 3 * KT).then_inc(acc_full, 1)
                    if after:
                        after(lt)
                return m

            def by_channels(b, hi, lo, kts, width):
                m = SPLIT_AT[b]
                pe.wait_ge(w_lo_done, m + 1)
                wh = wt_hi[:, m % SPLIT_T, :].rearrange("p (k f) -> p k f", k=kts)
                wl = wt_lo[:, m % SPLIT_T, :].rearrange("p (k f) -> p k f", k=kts)
                for cc in range(width // P):
                    cs = slice(cc * P, (cc + 1) * P)
                    for f in range(2):
                        o = acc(b + (cc, f))[:, 0:HALF]
                        fs = slice(f * HALF, (f + 1) * HALF)
                        pairs = [pr for k in range(kts) for pr in (
                            (wh[:, k, cs], hi[:, k, fs]), (wh[:, k, cs], lo[:, k, fs]), (wl[:, k, cs], hi[:, k, fs]))]
                        three(o, pairs, 3 * kts).then_inc(acc_full, 1)

            pe.wait_ge(s_cond, 16 * 9)
            transpose(tr(("vec", 0, 0))[:, 0:N_VEC], vec_rows[:]).then_inc(tr_full, 1)
            pe.wait_ge(s_scond, 1)
            for b in range(8):
                ada(b)
            for lt in range(NT):
                pe.wait_ge(s_xn, lt + 1)
                for i in range(2):
                    o = tr(("h", lt, i))
                    for a in range(4):
                        k = 4 * i + a
                        ins = transpose(o[:, a * P:(a + 1) * P], xn[:, lt % 2, k * P:(k + 1) * P])
                    ins.then_inc(tr_full, 1)

            def qk_transpose(s):
                kind, i = SPLITS[s // NT]
                lt = s % NT
                pe.wait_ge(s_rope, s + 1)
                o = tr(("t", kind, i, lt))
                for a in range(2):
                    src = q_rope[:, s % 2, a * P:(a + 1) * P] if kind == "q" else k_n[:, lt, i * 256 + a * P:i * 256 + (a + 1) * P]
                    ins = transpose(o[:, a * P:(a + 1) * P], src)
                ins.then_inc(tr_full, 1)

            for m in range(8):
                b = SPLITS[m]

                def after(lt, m=m):
                    s = m * NT + lt - 1
                    if 0 <= s < 4 * NT and m < 4:
                        qk_transpose(s)

                by_tokens(b, act_hi, act_lo, after if m < 4 else None)
                if m == 3:
                    qk_transpose(4 * NT - 1)

            def on_transpose(h):
                for lt in range(NT):
                    pe.wait_ge(s_on, NT * h + lt + 1)
                    o = tr(("on", h, lt))
                    for a in range(2):
                        ins = transpose(o[:, a * P:(a + 1) * P], o_raw[:, lt, a * P:(a + 1) * P])
                    ins.then_inc(tr_full, 1)

            pe.wait_ge(acc_read["act"], 8 * NT)
            pe.wait_ge(tr_read["act"], 4 * NT + 1)
            pe.wait_ge(s_ada0, 1)
            for h in range(H):
                pe.wait_ge(s_kdec, 2 * h + 2)
                for u in [("kvf", h, lt) for lt in (0, 1, 2)] + [("kvb", h, lt) for lt in (3, 2, 1)] + [("kvf", h, 4), ("kvb", h, 4)]:
                    lt = u[2]
                    k = (kb if u[0] == "kvb" else kf)[:, lt, :]
                    o = acc(u)[:, 0:DV]
                    mm(o, k, v_n[:, lt, h * DV:(h + 1) * DV], start=True, stop=True).then_inc(acc_full, 1)
                if h:
                    on_transpose(h - 1)
                for b in range(8 + 4 * h, 12 + 4 * h):
                    ada(b)
                pe.wait_ge(s_qdec, 2 * h + 2)
                pe.wait_ge(s_state, 6 * h + 6)
                for lt in range(NT + 1):
                    if lt < NT:
                        sl = slice(lt * P, (lt + 1) * P)
                        mm(acc(("sc", h, lt))[:, 0:P], k_t[:, h, sl], q_t[:, h, sl], start=True, stop=True).then_inc(acc_full, 1)
                    if lt:
                        t = lt - 1
                        o = acc(("o", h, t))[:, 0:DV]
                        pe.wait_ge(acc_read["dve"], DVE_READ["sc", h, t])
                        ins = mm(o, probs[:, (NT * h + t) % 2, :], v_n[:, t, h * DV:(h + 1) * DV], start=True, stop=t == NS)
                        if t < NS:
                            mm(o, qf[:, t, :], s0[:, h % 2, 0, :] if t == 0 else states[:, t - 1, :], start=False, stop=False)
                            ins = mm(o, qb[:, t, :], s0[:, h % 2, 1, :] if t == 3 else states[:, 3 + 2 - t, :],
                                     start=False, stop=True)
                        ins.then_inc(acc_full, 1)
            pe.wait_ge(s_ada, 1)
            transpose(tr(("ada", 0, 0))[0:96, 0:P], ada_t[:].rearrange("p a b -> p (a b)")).then_inc(tr_full, 1)
            for m in range(8, 28):
                b = SPLITS[m]
                kind, i = b
                if b == ("ro", 0):
                    pe.wait_ge(s_glo, 16)
                if b == ("sp", 0):
                    pe.wait_ge(s_pooled, 1)
                    pe.wait_ge(s_const, 16 * N_CONST)
                    for g in range(4):
                        for f in range(2):
                            mm(acc(("pg", g, f))[:, 0:HALF], wp_sb[:, g, :], pooled[:, g, f * HALF:(f + 1) * HALF],
                               start=True, stop=True).then_inc(acc_full, 1)
                if b == ("po", 0):
                    pe.wait_ge(s_glo, 24)
                hi, lo = {"ro": (ret_hi, ret_lo), "po": (py_hi, py_lo)}.get(kind, (act_hi, act_lo))
                by_channels(b, hi, lo, 4 if kind == "po" else KT, 512 if kind == "po" else 256)
                if b == ("g", 0):
                    on_transpose(H - 1)
            pe.wait_ge(s_glo, 40)
            for i in range(4):
                by_tokens(("wo", i), act_hi, act_lo)
            for lt in range(NT):
                pe.wait_ge(s_h2, lt + 1)
                if lt == 0:
                    pe.wait_ge(s_const, 16 * N_CONST)
                for i in range(2):
                    o = tr(("h2", lt, i))
                    for a in range(4):
                        k = 4 * i + a
                        ins = transpose(o[:, a * P:(a + 1) * P], h2[:, lt % 2, k * P:(k + 1) * P])
                        if k == 0 and lt == 0:
                            ins.then_inc(e_used, SPLIT_E)
                    ins.then_inc(tr_full, 1)
                o = tr(("lg", lt, 0))
                pe.wait_ge(tr_read["act"], TR_READ_H2[lt])
                for k in range(KT):
                    ins = mm(o[:, 0:NE], h2_t[:, lt % 2, k * P:(k + 1) * P], wr_sb[:, k, :], start=k == 0, stop=k == KT - 1)
                ins.then_inc(tr_full, 1)
                pe.wait_ge(s_aff, lt + 1)
                transpose(tr(("af", lt, 0))[0:NE, 0:P], aff[:, lt % 2, :]).then_inc(tr_full, 1)
            pe.wait_ge(s_top, CAP // 8 + 1)
            transpose(tr(("ix", 0, 0))[0:CAP, 0:NE], top_f[:]).then_inc(tr_full, 1)
            transpose(tr(("ga", 0, 0))[0:CAP, 0:NE], top_v[:]).then_inc(tr_full, 1)

            def group(e, g):
                if g >= NJ:
                    pe.wait_ge(e_gath, 16 * e + 32)
                else:
                    pe.wait_ge(e_hid, NJ * e + NJ + g + 1)
                if not (isinstance(e, int) and e < 0):
                    pe.wait_ge(e_tr_split, NG * e + NG + g - 1)
                n = 4 if g >= NJ else TILE_EDGE[g % 4 + 1] - TILE_EDGE[g % 4]
                for i in range(n):
                    t = 4 * (g - NJ) + i if g >= NJ else TILE_EDGE[g % 4] + i
                    src = (x_rows if g >= NJ else hid)[:, t * P:(t + 1) * P]
                    ins = transpose(bank[5 + g % 2][:, i * CAP:(i + 1) * CAP], src)
                ins.then_inc(e_tr, NJ + 1 if isinstance(e, int) and e < 0 and g == NJ else 1)

            pe.wait_ge(s_idx, 2)
            group(-1, NJ)
            group(-1, NJ + 1)

            def expert(e, last):
                for n in range(NB):
                    j = n // 2
                    pe.wait_ge(e_lo, e * NB + n + 1 + RAW_E)
                    wh, wl = we_hi[:, n % SPLIT_E, :], we_lo[:, n % SPLIT_E, :]
                    if n < 2 * NJ:
                        if n == 0:
                            pe.wait_ge(e_tr_split, NG * e + NG)
                        if n % 2 == 0:
                            pe.wait_ge(e_silu, NJ * e + NJ + j - 1)
                        else:
                            pe.wait_ge(e_hid, NJ * e + NJ + j - 1)
                        o = bank[2 * (n % 2) + j % 2][0:CAP, 0:FB]
                        wh, wl = (w.rearrange("p (k f) -> p k f", k=KT) for w in (wh, wl))
                        pairs = [pr for k in range(KT) for pr in (
                            (xs_hi[:, k, :], wh[:, k, :]), (xs_lo[:, k, :], wh[:, k, :]), (xs_hi[:, k, :], wl[:, k, :]))]
                        three(o, pairs, 3 * KT).then_inc(e_used, 1)
                    else:
                        q, part = (n - 2 * NJ) // 2, n % 2
                        if part == 0:
                            pe.wait_ge(e_out, NQ * e + NQ + q - 1)
                        if q == 0:
                            pe.wait_ge(e_tr_split, NG * e + NG + 4 + 4 * part)
                        o = bank[DOWN_BANK[q % 2]][0:CAP, 0:DQ]
                        wh, wl = (w.rearrange("p (k f) -> p k f", k=FTH) for w in (wh, wl))
                        for i in range(FTH):
                            t = part * FTH + i
                            for z, (a, b) in enumerate(((hd_hi, wh), (hd_lo, wh), (hd_hi, wl))):
                                ins = mm(o, a[:, t, :], b[:, i, :], start=t == 0 and z == 0, stop=t == FT - 1 and z == 2)
                        ins.then_inc(e_used, 1)
                    if n in TR_AFTER:
                        g = TR_AFTER[n]
                        if g < NJ or not last:
                            group(e, g)

            with pe.Fori(0, NE - 1) as e:
                expert(e, False)
            expert(NE - 1, True)


DOWN_BANK = (4, 7)
TR_AFTER = {**{2 * g + 2: g for g in range(NJ)}, 2 * NJ + 3: NJ, 2 * NJ + 4: NJ + 1}
N_CONST = 6
N_VEC = 108


def _counts(units, engine):
    out, n = {}, 0
    for u, e in units:
        if e == engine:
            n += 1
            out[u] = n
    return out


LAST_UNIT = {b: max(ACC.full(u) for u in ACC.at if u[:2] == b and len(u) > 2) for b in SPLITS}
ACT_READ = _counts(acc_units(), "act")
DVE_READ = _counts(acc_units(), "dve")
TR_ACT = _counts(tr_units(), "act")
ACT_READ_U = [ACT_READ["u", g // 2, g % 2, 1] for g in range(4)]
ACT_READ_O = {(h, lt): ACT_READ["o", h, lt] for h in range(H) for lt in range(NT)}
ACT_READ_G = [ACT_READ["g", z // 4, z // 2 % 2, z % 2] for z in range(16)]
ACT_READ_SR = ACT_READ["sr", 3, 1, 1]
ACT_READ_SP = ACT_READ["sp", 3, 1, 1]
DVE_READ_RO = DVE_READ["ro", 3, 1, 1]
TR_READ_ON = [TR_ACT["on", h, NT - 1] for h in range(H)]
TR_READ_AF = TR_ACT["af", NT - 1, 0]
TR_READ_H2 = [TR_ACT["h2", lt, 1] for lt in range(NT)]


_INS = ["x_prompt", "x_sample", "c", "state_ret", "c_ctx", "w_ada", "b_ada", "norm1_g", "w_in", "w_pool", "pool_scale",
        "w_pool_out", "ret_decay", "ret_gn_g", "w_ret_out", "w_branch_gate", "b_branch_gate", "w_out", "norm2_g",
        "w_router", "w_exp_gate", "w_exp_up", "w_exp_down", "final_norm_g"]
_OUTS = [(1, L_P, D), (1, L_S, D), (1, 1, 2, H, DK, DV)]


def kernel(**inputs):
    import concourse.bacc as bacc
    from concourse.bass_utils import run_bass_kernel_spmd as run

    nc = bacc.Bacc("TRN2", target_bir_lowering=False, num_devices=1)
    arrays, args = {}, []
    for name in _INS:
        a = np.ascontiguousarray(inputs[name])
        arrays[f"in_{name}_dram"] = a
        args.append(nc.dram_tensor(f"in_{name}_dram", a.shape, mybir.dt.from_np(a.dtype), kind="ExternalInput").ap())
    arrays["tables_dram"] = shape_tables()
    args.append(nc.dram_tensor("tables_dram", (P, C_END), F32, kind="ExternalInput").ap())
    for i, shape in enumerate(_OUTS):
        args.append(nc.dram_tensor(f"out_{i}_dram", shape, F32, kind="ExternalOutput").ap())
    build(nc, *args)
    r = run(nc, [arrays], core_ids=[0])
    return tuple(r.results[0][f"out_{i}_dram"] for i in range(len(_OUTS)))
```

```python
import numpy as np
import concourse.bass as bass
from concourse import mybir
from contextlib import ExitStack

F32 = mybir.dt.float32
F32R = mybir.dt.float32r
I32 = mybir.dt.int32
U32 = mybir.dt.uint32
ALU = mybir.AluOpType
ACT = mybir.ActivationFunctionType
AX = mybir.AxisListType

P = 128
D = 1024
KT = D // P
L_S, L_P = 512, 128
NS = L_S // P
NT = NS + 1
T = L_S + L_P
HALF = T // 2
POOL_W = 512
WINDOWS = (2, 4, 8, 16)
H = 4
DK = 128
DV = 256
NE = 16
FF = 2816
C_S, C_P = 2 * L_S // NE, 2 * L_P // NE
CAP = C_S + C_P
GRID_W = 64
EPS = 1e-6

WB = 2048
RAW_T = 3
SPLIT_T = 2

FB = 352
NJ = FF // FB
DQ = 256
NQ = D // DQ
FT = FF // P
FTH = FT // 2
EB = KT * FB
assert EB == FTH * DQ
NB = 2 * NJ + 2 * NQ
RAW_E = 4
SPLIT_E = 3
AHEAD = 2
TILE_EDGE = (0, 2, 5, 8, 11)
NG = NJ + 2

C_ID, C_DPL, C_DMI, C_QF, C_QB, C_KP, C_COS, C_SIN, C_EDGE, C_END = (
    0, 128, 256, 384, 512, 640, 642, 642 + 512, 642 + 1024, 642 + 1024 + 64)


def shape_tables():
    i = np.arange(P, dtype=np.float32)
    t = np.zeros((P, C_END), np.float32)
    t[:, C_ID:C_ID + P] = np.eye(P, dtype=np.float32)
    diff = i[None, :] - i[:, None]
    t[:, C_DPL:C_DPL + P] = np.maximum(diff, 0)
    t[:, C_DMI:C_DMI + P] = np.maximum(-diff, 0)
    t[:, C_QF:C_QF + P] = i[None, :] + 1
    t[:, C_QB:C_QB + P] = P - i[None, :]
    t[:, C_KP] = P - 1 - i
    t[:, C_KP + 1] = i
    nf = DK // 4
    inv = (np.float32(10000.0) ** (-np.arange(nf, dtype=np.float32) / np.float32(nf))).astype(np.float32)
    tok = np.arange(L_S)
    row, col = (tok // GRID_W).astype(np.float32), (tok % GRID_W).astype(np.float32)
    ang = np.concatenate([row[:, None] * inv, col[:, None] * inv], axis=-1).astype(np.float32)
    cos, sin = np.cos(ang), np.sin(ang)
    full_c = np.repeat(cos, 2, axis=1)
    full_s = np.stack([-sin, sin], axis=-1).reshape(L_S, DK)
    t[:, C_COS:C_COS + 512] = full_c.reshape(NS, P, DK).transpose(1, 0, 2).reshape(P, -1)
    t[:, C_SIN:C_SIN + 512] = full_s.reshape(NS, P, DK).transpose(1, 0, 2).reshape(P, -1)
    for g, w in enumerate(WINDOWS):
        for e in range(8):
            t[:, C_EDGE + 16 * g + e] = w / min(w, e + w // 2)
            t[:, C_EDGE + 16 * g + 8 + e] = w / min(w, 8 - e + w // 2)
    return t


def trunk_blocks():
    ada = [("ada", b) for b in range(24)]
    return (ada[:8] + [("q", 0), ("q", 1), ("k", 0), ("k", 1)] + [("v", b) for b in range(4)] + ada[8:]
            + [("g", b) for b in range(4)] + [("u", 0), ("u", 1)] + [("sr", b) for b in range(4)]
            + [("ro", b) for b in range(4)] + [("sp", b) for b in range(4)] + [("po", 0), ("po", 1)]
            + [("wo", b) for b in range(4)])


BLOCKS = trunk_blocks()
INDEX = {b: n for n, b in enumerate(BLOCKS)}
QKV = BLOCKS[8:16]
BRANCH = BLOCKS[32:]



def acc_units():
    out = []
    out += [(("ada", b, 0), "act") for b in range(8)]
    for b in QKV:
        out += [(b + (lt,), "act") for lt in range(NT)]
    for h in range(H):
        out += [(("kvf", h, lt), "state") for lt in (0, 1, 2)] + [(("kvb", h, lt), "state") for lt in (3, 2, 1)]
        out += [(("kvf", h, 4), "dve"), (("kvb", h, 4), "dve")]
        for lt in range(NT + 1):
            if lt < NT:
                out.append((("sc", h, lt), "dve"))
            if lt:
                out.append((("o", h, lt - 1), "act"))
            if lt < 4:
                out.append((("ada", 8 + 4 * h + lt, 0), "act"))
    for b in BRANCH:
        if b == ("sp", 0):
            out += [(("pg", g, f), "product") for g in range(4) for f in range(2)]
        if b[0] == "wo":
            out += [(b + (lt,), "dve") for lt in range(NT)]
        else:
            engine = "act" if b[0] in ("g", "u", "sr", "sp") else "dve"
            n = 4 if b[0] == "po" else 2
            out += [(b + (c, f), engine) for c in range(n) for f in range(2)]
    return out


def tr_units():
    out = [(("vec", 0, 0), "act"), (("h", 0, 0), "h"), (("h", 0, 1), "h")]
    for b in QKV[:4]:
        for lt in range(NT):
            if b == QKV[0] and lt + 1 < NT:
                out += [(("h", lt + 1, i), "h") for i in range(2)]
            s = QKV.index(b) * NT + lt - 1
            if s >= 0:
                out.append((("t",) + QKV[s // NT] + (s % NT,), "act"))
    out.append((("t",) + QKV[3] + (NT - 1,), "act"))
    for h in range(H):
        if h:
            out += [(("on", h - 1, lt), "act") for lt in range(NT)]
    out += [(("ada", 0, 0), "act")]
    out += [(("on", H - 1, lt), "act") for lt in range(NT)]
    for lt in range(NT):
        out += [(("h2", lt, 0), "act"), (("h2", lt, 1), "act")]
    out += [(("af", 0, 0), "act"), (("af", 1, 0), "act")]
    out += [(("ix", 0, 0), "dve"), (("ga", 0, 0), "dve")]
    return out


class Plan:

    def __init__(self, units, banks):
        self.at = {u: i for i, (u, _) in enumerate(units)}
        self.engine = [e for _, e in units]
        self.banks = banks
        self.n = len(units)

    def bank(self, u):
        return self.banks[self.at[u] % len(self.banks)]

    def full(self, u):
        return self.at[u] + 1

    def previous(self, u):
        i = self.at[u] - len(self.banks)
        if i < 0:
            return None
        n = sum(e == self.engine[i] for e in self.engine[:i + 1])
        if self.engine[i] == "h":
            n *= 4
        if self.engine[i] == "product":
            n += 16
        return self.engine[i], n


ACC = Plan(acc_units(), (0, 1, 2, 3, 4))
TR = Plan(tr_units(), (5, 6))


def build(nc, x_prompt, x_sample, c, state_ret, c_ctx, w_ada, b_ada, norm1_g, w_in, w_pool, pool_scale,
          w_pool_out, ret_decay, ret_gn_g, w_ret_out, w_branch_gate, b_branch_gate, w_out, norm2_g,
          w_router, w_exp_gate, w_exp_up, w_exp_down, final_norm_g, tables, y_prompt, y_sample, new_state):
    ctx = ExitStack()
    with ctx:
        base = 16512

        def at(name, offset, shape, dt=F32):
            return nc.alloc_sbuf_tensor_at(name, shape, dt, offset=base + offset)

        A, X, CC, RT, HT, M0 = 0, 45056, 65536, 116736, 141312, 174080
        act_hi, act_lo = at("act_hi", A, [P, KT, T], F32R), at("act_lo", A + 20480, [P, KT, T], F32R)
        cos_t, sin_t = at("cos_t", A + 40960, [P, NS, DK]), at("sin_t", A + 43008, [P, NS, DK])
        x_in = at("x_in", X, [P, NT, D])
        o_t = at("o_t", X, [P, KT, T])
        mix = at("mix", X, [P, KT, T])
        x2 = at("x2", X, [P, NT, D])
        x_sq = at("x_sq", CC, [P, D])
        xn = at("xn", CC + 22528, [P, 2, D])
        q_rope = at("q_rope", X + 2048, [P, 2, 256])
        probs = at("probs", A + 40960, [P, 2, P])
        rope_tmp = at("rope_tmp", X, [P, 256])
        h_tmp = at("h_tmp", CC + 30720, [P, 4, 512])
        q_t, k_t = at("q_t", CC, [P, H, T]), at("k_t", CC + 10240, [P, H, T])
        k_n = at("k_n", CC + 20480, [P, NT, H * DK])
        v_n = at("v_n", CC + 30720, [P, NT, H * DV])
        ret_hi, ret_lo = at("ret_hi", CC, [P, KT, T], F32R), at("ret_lo", CC + 20480, [P, KT, T], F32R)
        pooled = at("pooled", CC + 40960, [P, 4, T])
        py_hi, py_lo = at("py_hi", CC, [P, 4, T], F32R), at("py_lo", CC + 10240, [P, 4, T], F32R)
        sig_p = at("sig_p", CC + 20480, [P, KT, T])
        raw_t = at("raw_t", RT, [P, RAW_T, WB])
        wt_hi, wt_lo = at("wt_hi", HT, [P, SPLIT_T, WB], F32R), at("wt_lo", HT + 16384, [P, SPLIT_T, WB], F32R)

        place = [M0]

        def misc(name, shape, dt=F32, alias=None):
            size = int(np.prod(shape[1:])) * 4
            size += -size % 32
            if alias is not None:
                return at(name, alias, shape, dt)
            place[0] += size
            return at(name, place[0] - size, shape, dt)

        ident = misc("ident", [P, P])
        ada_t = misc("ada_t", [P, 48, 2])
        vec_rows = at("vec_rows", CC, [N_VEC, P])
        cols = misc("cols", [P, N_VEC])
        n1g, n2g, gng, pscale, bbg, bada = (cols[:, a:b] for a, b in (
            (16, 24), (24, 32), (32, 40), (40, 44), (44, 60), (60, 108)))
        scond = misc("scond", [P, 2, KT])
        sc_hi, sc_lo = misc("sc_hi", [P, 2, KT], F32R), misc("sc_lo", [P, 2, KT], F32R)
        ada_row_sb = [at(f"ada_row_sb{i}", o, [2, 2, 256]) for i, o in enumerate((CC + 20480, A + 41984))]
        gs1 = misc("gs1", [P, KT, 2])
        lgam = misc("lgam", [P, 2, H])
        kdec = misc("kdec", [P, 2, H])
        cdec = misc("cdec", [P, 2, H])
        kpow = misc("kpow", [P, 2])
        edge = misc("edge", [P, 4, 16])
        mv = misc("mv", [P, NT, 2])
        small = misc("small", [P, 64])
        wr_sb = misc("wr_sb", [P, KT, NE])
        wp_sb = misc("wp_sb", [P, 4, P])
        dead = place[0]
        mask = misc("mask", [P, H, P])
        qfp, qbp = misc("qfp", [P, H, P]), misc("qbp", [P, H, P])
        qk_raw = misc("qk_raw", [P, 2, 256])
        kf, kb = misc("kf", [P, NT, P]), misc("kb", [P, NT, P])
        qf, qb = misc("qf", [P, NS, P]), misc("qb", [P, NS, P])
        s0 = misc("s0", [P, 2, 2, DV])
        states = misc("states", [P, 6, DV])
        o_raw = place[0]
        pows = misc("pows", [P, 4, P], alias=o_raw)
        o_raw = misc("o_raw", [P, NT, DV])
        assert base + place[0] <= 229344, place[0]
        pool_a = at("pool_a", dead, [P, 2, 544])
        gtmp = at("gtmp", dead + 4352, [P, 2, HALF])
        rtmp = at("rtmp", dead + 6912, [P, 2, HALF])
        g1_b = at("g1_b", dead + 9472, [P, 2, D])
        gs2_b = at("gs2_b", dead + 17664, [P, 2, D])
        adar = at("adar", dead + 25856, [96, P])
        assert dead + 25856 + 512 <= 229344 - base
        h2 = at("h2", RT, [P, 3, D])
        h2_t = at("h2_t", RT + 12288, [P, 2, D])
        x2_sq = at("x2_sq", RT + 20480, [P, D])
        sh2_b = [at("sh2_sample", A + 40960, [P, D]), at("sh2_prompt", dead, [P, D])]
        lg_t = at("lg_t", HT + 29056, [NE, T])
        aff = at("aff", HT + 28672, [P, NT, NE])
        aff_t = at("aff_t", HT, [NE, 2, T])
        top_v = at("top_v", HT + 5120, [NE, CAP])
        top_i = at("top_i", HT + 5504, [NE, CAP], U32)
        top_f = at("top_f", HT + 5888, [NE, CAP])
        idx_all = at("idx_all", HT + 6272, [CAP, NE], I32)
        gate_all = at("gate_all", HT + 6336, [CAP, NE])
        raw_e = at("raw_e", CC, [P, RAW_E, EB])
        we_hi = [at(f"we_hi{i}", o, [P, EB], F32R) for i, o in enumerate((A, A + 11264, HT + 12288))]
        we_lo = [at(f"we_lo{i}", o, [P, EB], F32R) for i, o in enumerate((A + 22528, A + 33792, dead + 9472))]
        xs_hi, xs_lo = at("xs_hi", X, [P, KT, CAP], F32R), at("xs_lo", X + 2560, [P, KT, CAP], F32R)
        x_rows = at("x_rows", X + 5120, [CAP, D])
        out_rows = at("out_rows", X + 9216, [CAP, D])
        g2_rows = at("g2_rows", X + 13312, [CAP, D])
        silu_g = at("silu_g", X + 17408, [CAP, 2, FB])
        hid = at("hid", HT + 6400, [CAP, 4 * FB])
        hd_hi, hd_lo = at("hd_hi", RT, [P, FT, CAP], F32R), at("hd_lo", RT + 7040, [P, FT, CAP], F32R)
        gate_cur = at("gate_cur", HT + 12160, [CAP, 1])
        idx_gather = at("idx_gather", HT + 12192, [CAP, 1], I32)
        idx_scatter = at("idx_scatter", HT + 12224, [CAP, 1], I32)
        fg_b = at("fg_b", dead + 26400, [P, D])
        assert dead + 26400 + 4096 <= 229344 - base, dead
        y_tile = at("y_tile", CC, [P, NT, D])
        y_sq = at("y_sq", CC + 20480, [P, D])

        bank = [ctx.enter_context(nc.psum_tensor(f"bank{i}", [P, 512], F32)) for i in range(8)]
        ada_ps = bank[7]

        h2_dram = nc.dram_tensor("h2_scratch", (T, D), F32, kind="Internal").ap()
        acc_dram = nc.dram_tensor("acc_scratch", (T, D), F32, kind="Internal").ap()
        ada_dram = nc.dram_tensor("ada_scratch", (96, P), F32, kind="Internal").ap()

        def sem(name):
            return ctx.enter_context(nc.semaphore(name))

        s_x = [sem(f"s_x{i}") for i in range(NT)]
        s_cond, s_const, s_decay, s_s0 = sem("s_cond"), sem("s_const"), sem("s_decay"), [sem("s_s0a"), sem("s_s0b")]
        s_pow = sem("s_pow")
        w_landed = [sem(f"w_landed{i}") for i in range(RAW_T)]
        w_hi_done, w_lo_done, ada_done = sem("w_hi_done"), sem("w_lo_done"), sem("ada_done")
        acc_full = sem("acc_full")
        acc_read = {"act": sem("acc_read_act"), "dve": sem("acc_read_dve")}
        tr_full = sem("tr_full")
        tr_read = {"act": sem("tr_read_act"), "dve": sem("tr_read_dve")}
        s_scond, s_ada0, s_ada, s_gs = sem("s_scond"), sem("s_ada0"), sem("s_ada"), sem("s_gs")
        s_x2, s_fg = sem("s_x2done"), sem("s_fg")
        s_ms, s_sqrt, s_rstd, s_xn = sem("s_ms"), sem("s_sqrt"), sem("s_rstd"), sem("s_xn")
        s_htmp, s_hhi, s_hlo = sem("s_htmp"), sem("s_hhi"), sem("s_hlo")
        tr_read["h"] = s_htmp
        s_rope = sem("s_rope")
        s_exp, s_lgam, s_marg, s_tab = sem("s_exp"), sem("s_lgam"), sem("s_marg"), sem("s_tab")
        s_kdec, s_qdec = sem("s_kdec"), sem("s_qdec")
        s_state, s_outst, s_stdma = sem("s_state"), sem("s_outst"), sem("s_stdma")
        s_mv, s_osq, s_on = sem("s_mv"), sem("s_osq"), sem("s_on")
        s_adar, s_adaw, s_bc = sem("s_adar"), sem("s_adaw"), sem("s_bc")
        s_gsil, s_gmul, s_ghi, s_glo = sem("s_gsil"), sem("s_gmul"), sem("s_ghi"), sem("s_glo")
        acc_read["state"], acc_read["product"] = s_state, s_gmul
        s_pool, s_pooled = sem("s_pool"), sem("s_pooled")
        s_x2in = [sem(f"s_x2in{i}") for i in range(NT)]
        s_mixfree = sem("s_mixfree")
        dve_step, act_step = sem("dve_step"), sem("act_step")
        s_sh2, s_lg, s_lgt, s_lg_rows = sem("s_sh2"), sem("s_lg"), sem("s_lgt"), sem("s_lg_rows")
        s_h2, s_h2w, s_acc = sem("s_h2"), [sem(f"s_h2w{i}") for i in range(NT)], sem("s_acc")
        s_rmax, s_rexp, s_aff = sem("s_rmax"), sem("s_rexp"), sem("s_aff")
        s_top, s_idx = sem("s_top"), sem("s_idx")
        e_landed = [sem(f"e_landed{i}") for i in range(RAW_E)]
        e_hi, e_lo, e_used = sem("e_hi"), sem("e_lo"), sem("e_used")
        e_silu, e_hid, e_tr, e_tr_hi, e_tr_split = (sem(n) for n in ("e_silu", "e_hid", "e_tr", "e_tr_hi", "e_tr_split"))
        s_hold = sem("s_hold")
        e_out, e_idx, e_gath, s_g2 = sem("e_out"), sem("e_idx"), sem("e_gath"), sem("s_g2")
        s_fin, s_y, s_out = [sem(f"s_fin{i}") for i in range(NT)], sem("s_y"), sem("s_out")

        block = ctx.enter_context(nc.Block())

        def x_dram(lt):
            return x_sample[0, lt * P:(lt + 1) * P, :] if lt < NS else x_prompt[0]

        def w_source(b):
            kind, i = b
            col = {"ada": 0, "u": 0, "q": 512, "k": 1024, "v": 1536, "g": 2560, "sr": D, "ro": 0, "sp": 0, "wo": 0}
            mat = {"ada": w_ada, "sr": w_branch_gate, "sp": w_branch_gate, "ro": w_ret_out, "wo": w_out}
            if kind == "po":
                return w_pool_out[0, :, i * 512:(i + 1) * 512].rearrange("(k p) f -> p k f", p=P), 512
            m = mat.get(kind, w_in)
            o = col[kind] + 256 * i
            return m[0, :, o:o + 256].rearrange("(k p) f -> p k f", p=P), 256

        def wait_raw_free(eng, n):
            if n >= RAW_T:
                eng.wait_ge(w_lo_done, n - RAW_T + 1)

        def e_block(n):
            if n < 2 * NJ:
                return (w_exp_gate, w_exp_up)[n % 2], n // 2
            return w_exp_down, n - 2 * NJ

        @block.sync
        def _(sp):
            sp.dma_start(ident[:], tables[:, C_ID:C_ID + P]).then_inc(s_cond, 16)
            row = 0
            for v in (c[0], c_ctx, norm1_g[0], norm2_g[0], ret_gn_g[0], pool_scale[0], b_branch_gate[0], b_ada[0]):
                n = v.shape[0] // P
                sp.dma_start(vec_rows[row:row + n, :], v.rearrange("(k p) -> k p", p=P)).then_inc(s_cond, 16)
                row += n
            assert row == N_VEC
            for n, b in enumerate(BLOCKS):
                wait_raw_free(sp, n)
                src, width = w_source(b)
                sp.dma_start(raw_t[:, n % RAW_T, :].rearrange("p (k f) -> p k f", f=width), src)\
                  .then_inc(w_landed[n % RAW_T], 16)
            with sp.Fori(0, NE) as e:
                for n in range(NB):
                    sp.wait_ge(e_lo, e * NB + n + 1)
                    m, j = e_block(n)
                    slot = raw_e[:, n % RAW_E, :]
                    if n < 2 * NJ:
                        src = m[0, bass.ds(e, 1), :, j * FB:(j + 1) * FB].rearrange("a (k p) f -> p (a k) f", p=P)
                        dst = slot.rearrange("p (k f) -> p k f", f=FB)
                    else:
                        q, part = j // 2, j % 2
                        src = m[0, bass.ds(e, 1), part * FTH * P:(part + 1) * FTH * P, q * DQ:(q + 1) * DQ]\
                            .rearrange("a (k p) f -> p (a k) f", p=P)
                        dst = slot.rearrange("p (k f) -> p k f", f=DQ)
                    sp.dma_start(dst, src).then_inc(e_landed[n % RAW_E], 16)
            sp.wait_ge(s_acc, 16 * NT + 16 * NE)
            for lt in range(NT):
                sp.dma_start(y_tile[:, lt, :], acc_dram[lt * P:(lt + 1) * P, :]).then_inc(s_fin[lt], 16)
            for lt in range(NT):
                sp.wait_ge(s_y, lt + 1)
                dst = y_sample[0, lt * P:(lt + 1) * P, :] if lt < NS else y_prompt[0]
                sp.dma_start(dst, y_tile[:, lt, :]).then_inc(s_out, 16)
            sp.wait_ge(s_out, 16 * NT)
            sp.wait_ge(s_stdma, 16 * 2 * H)

        @block.gpsimd
        def _(pool):
            for lt in range(NT):
                pool.dma_start(x_in[:, lt, :], x_dram(lt)).then_inc(s_x[lt], 16)
            n_const = 0
            for dst, src in (
                (cos_t[:].rearrange("p a b -> p (a b)"), tables[:, C_COS:C_COS + 512]),
                (sin_t[:].rearrange("p a b -> p (a b)"), tables[:, C_SIN:C_SIN + 512]),
                (kpow[:], tables[:, C_KP:C_KP + 2]), (edge[:].rearrange("p a b -> p (a b)"), tables[:, C_EDGE:C_END]),
                (wr_sb[:], w_router[0].rearrange("(k p) e -> p k e", p=P)),
                (wp_sb[:], w_pool[0].rearrange("g c d -> c g d")),
            ):
                pool.dma_start(dst, src).then_inc(s_const, 16)
                n_const += 1
            assert n_const == N_CONST
            pool.dma_start(lgam[:].rearrange("p a b -> p (a b)"),
                           ret_decay[0:1].rearrange("a d h -> a (d h)").to_broadcast([P, 2 * H])).then_inc(s_decay, 16)
            pool.dma_start(pows[:].rearrange("p a b -> p (a b)"), tables[:, C_DPL:C_DPL + 512]).then_inc(s_pow, 16)
            for z in range(2 * NT):
                lt, i = divmod(z, 2)
                sl = slice(lt * P, (lt + 1) * P)
                pool.wait_ge(s_htmp, 4 * (z + 1))
                pool.wait_ge(s_hhi, z + 1)
                nc.gpsimd.tensor_tensor(act_lo[:, 4 * i:4 * i + 4, sl], h_tmp[:, z % 4, :].rearrange("p (a b) -> p a b", a=4),
                                        act_hi[:, 4 * i:4 * i + 4, sl].bitcast(F32), ALU.subtract).then_inc(s_hlo, 1)
            pool.wait_ge(s_tab, 10)

            def start_states(h):
                if h >= 2:
                    pool.wait_ge(acc_full, ACC.full(("o", h - 2, 4)))
                    pool.wait_ge(s_state, 6 * (h - 1))
                for d in range(2):
                    pool.dma_start(s0[:, h % 2, d, :], state_ret[0, 0, d, h]).then_inc(s_s0[h % 2], 16)

            def decayed_k(h):
                if h == 0:
                    pool.wait_ge(s_rope, 4 * NT)
                else:
                    pool.wait_ge(acc_full, ACC.full(("kvb", h - 1, 4)))
                ks = k_n[:, :, h * DK:(h + 1) * DK]
                nc.gpsimd.tensor_scalar(kf[:], ks, kdec[:, 0, h:h + 1], None, ALU.mult).then_inc(s_kdec, 1)
                nc.gpsimd.tensor_scalar(kb[:], ks, kdec[:, 1, h:h + 1], None, ALU.mult).then_inc(s_kdec, 1)

            start_states(0)
            start_states(1)
            decayed_k(0)
            for h in range(H):
                if h == 0:
                    pool.wait_ge(tr_read["act"], 4 * NT + 1)
                else:
                    pool.wait_ge(acc_full, ACC.full(("o", h - 1, 4)))
                qs = q_t[:, h, 0:L_S].rearrange("p (a b) -> p a b", a=NS)
                for dst, tab in ((qf, qfp), (qb, qbp)):
                    nc.gpsimd.tensor_tensor(dst[:], qs, tab[:, h, :].unsqueeze(1).to_broadcast([P, NS, P]),
                                            ALU.mult).then_inc(s_qdec, 1)
                if 1 <= h < H - 1:
                    start_states(h + 1)
                if h + 1 < H:
                    decayed_k(h + 1)
                pool.wait_ge(acc_read["dve"], DVE_READ["kvb", h, 4])
                for d in range(2):
                    pool.dma_start(new_state[0, 0, d, h], qk_raw[:, d, :]).then_inc(s_stdma, 16)
            pool.wait_ge(s_adar, 1)
            pool.dma_start(ada_dram, adar[:]).then_inc(s_adaw, 16)
            pool.wait_ge(s_adaw, 16)

            def ada_row(param, cond_i):
                return ada_dram.rearrange("(j s) p -> s j p", s=2)[cond_i:cond_i + 1, 8 * param:8 * param + 8, :]

            for cnd in range(2):
                pool.dma_start(g1_b[:, cnd, :].rearrange("p (j q) -> p j q", j=8),
                               ada_row(2, cnd).to_broadcast([P, 8, P])).then_inc(s_bc, 16)
                pool.dma_start(gs2_b[:, cnd, :].rearrange("p (j q) -> p j q", j=8),
                               ada_row(4, cnd).to_broadcast([P, 8, P])).then_inc(s_bc, 16)
            steps = 0
            pad = 8
            for g, w in enumerate(WINDOWS):
                pool.wait_ge(acc_read["act"], ACT_READ_U[g])
                for lo, n in ((0, L_S), (L_S, L_P)):
                    if g or lo:
                        pool.wait_ge(s_pool, steps)
                    for i in range(2):
                        nc.gpsimd.memset(pool_a[:, i, :], 0.0).then_inc(s_pool, 1)
                    steps += 2
                    pool.wait_ge(s_pool, steps)
                    u = pooled[:, g, lo:lo + n]
                    nc.gpsimd.tensor_copy(pool_a[:, 0, pad:pad + n], u).then_inc(s_pool, 1)
                    steps += 1
                    cur, span = 0, 1
                    while span < w:
                        pool.wait_ge(s_pool, steps)
                        m = n + 2 * pad - 2 * span + 1
                        nc.gpsimd.tensor_tensor(pool_a[:, 1 - cur, 0:m], pool_a[:, cur, 0:m],
                                                pool_a[:, cur, span:span + m], ALU.add).then_inc(s_pool, 1)
                        steps += 1
                        cur, span = 1 - cur, 2 * span
                    o = pad - w // 2
                    pool.wait_ge(s_pool, steps)
                    nc.gpsimd.tensor_tensor(pool_a[:, cur, o:o + 8], pool_a[:, cur, o:o + 8], edge[:, g, 0:8],
                                            ALU.mult).then_inc(s_pool, 1)
                    nc.gpsimd.tensor_tensor(pool_a[:, cur, o + n - 8:o + n], pool_a[:, cur, o + n - 8:o + n],
                                            edge[:, g, 8:16], ALU.mult).then_inc(s_pool, 1)
                    steps += 2
                    pool.wait_ge(s_pool, steps)
                    nc.gpsimd.tensor_scalar(pool_a[:, cur, o:o + n], pool_a[:, cur, o:o + n], 1.0 / w, None,
                                            ALU.mult).then_inc(s_pool, 1)
                    steps += 1
                    pool.wait_ge(s_pool, steps)
                    nc.gpsimd.tensor_tensor(u, pool_a[:, cur, o:o + n], u, ALU.subtract).then_inc(s_pool, 1)
                    steps += 1
            pool.wait_ge(s_pool, steps)
            nc.gpsimd.memset(pool_a[:, 0, 0:1], 0.0).then_inc(s_pooled, 1)
            pool.wait_ge(s_pooled, 1)
            for cnd in range(2):
                pool.dma_start(sh2_b[cnd].rearrange("p (j q) -> p j q", j=8),
                               ada_row(3, cnd).to_broadcast([P, 8, P])).then_inc(s_sh2, 16)
            for y in range(24, 40):
                ct, f = divmod(y - 24, 2)
                pool.wait_ge(s_ghi, y + 1)
                nc.gpsimd.tensor_tensor(act_lo[:, ct, f * HALF:(f + 1) * HALF], rtmp[:, y % 2, :],
                                        act_hi[:, ct, f * HALF:(f + 1) * HALF].bitcast(F32), ALU.subtract).then_inc(s_glo, 1)
            pool.wait_ge(s_mixfree, 1)
            for lt in range(NT):
                pool.dma_start(x2[:, lt, :], x_dram(lt)).then_inc(s_x2in[lt], 16)
            for lt in range(NT):
                pool.wait_ge(s_h2, lt + 1)
                pool.dma_start(acc_dram[lt * P:(lt + 1) * P, :], x2[:, lt, :]).then_inc(s_acc, 16)
                pool.dma_start(h2_dram[lt * P:(lt + 1) * P, :], h2[:, lt % 3, :]).then_inc(s_h2w[lt], 16)
            pool.wait_ge(s_acc, 16 * NT)
            for lt in range(NT):
                pool.wait_ge(s_h2w[lt], 16)
            pool.dma_start(fg_b[:], final_norm_g.rearrange("(a n) -> a n", a=1).to_broadcast([P, D])).then_inc(s_fg, 16)
            for cnd, lo, n in ((0, 0, C_S), (1, C_S, C_P)):
                pool.dma_start(g2_rows[lo:lo + n, :].rearrange("p (j q) -> p j q", j=8),
                               ada_row(5, cnd).to_broadcast([n, 8, P])).then_inc(s_g2, 16)

            def hold():
                nc.gpsimd.tensor_tensor(small[:, 62:64], kpow[:], kpow[:], ALU.add).then_inc(s_hold, 1)

            def gather():
                pool.indirect_dma_start(x_rows[:], None, h2_dram, bass.IndirectOffsetOnAxis(idx_gather[:, 0:1], 0))\
                    .then_inc(e_gath, 16)

            def scatter():
                pool.indirect_dma_start(acc_dram, bass.IndirectOffsetOnAxis(idx_scatter[:, 0:1], 0), out_rows[:], None,
                                        compute_op=ALU.add).then_inc(s_acc, 16)

            pool.wait_ge(e_idx, 1)
            hold()
            gather()

            def expert(e, last):
                if not last:
                    pool.wait_ge(e_idx, 2 * e + 2)
                    pool.wait_ge(e_tr, NG * e + NG)
                    pool.wait_ge(s_hold, 2 * e + 1)
                    hold()
                    gather()
                pool.wait_ge(e_idx, 2 * e + 3 if not last else 2 * e + 2)
                pool.wait_ge(e_out, NQ * e + 2 * NQ)
                pool.wait_ge(s_hold, 2 * e + 2 if not last else 2 * e + 1)
                hold()
                scatter()

            with pool.Fori(0, NE - 1) as e:
                expert(e, False)
            expert(NE - 1, True)

        def qk_t(s, tr):
            kind, i = QKV[s // NT]
            lt = s % NT
            src = tr(("t", kind, i, lt))
            dst = (q_t if kind == "q" else k_t)[:, 2 * i:2 * i + 2, lt * P:(lt + 1) * P]
            nc.scalar.activation(dst, src[:, 0:256].rearrange("p (a b) -> p a b", a=2), ACT.Copy)\
              .then_inc(tr_read["act"], 1)

        def on_t(h, tr):
            for lt in range(NT):
                src = tr(("on", h, lt))
                nc.scalar.activation(o_t[:, 2 * h:2 * h + 2, lt * P:(lt + 1) * P],
                                     src[:, 0:256].rearrange("p (a b) -> p a b", a=2), ACT.Copy)\
                  .then_inc(tr_read["act"], 1)

        @block.scalar
        def _(act):
            steps = [0]

            def tick(ins):
                steps[0] += 1
                ins.then_inc(act_step, 1)
                act.wait_ge(act_step, steps[0])

            def split(m):
                if m >= len(BLOCKS):
                    return
                n = m
                act.wait_ge(w_landed[n % RAW_T], 16 * (n // RAW_T + 1))
                if m >= SPLIT_T:
                    act.wait_ge(acc_full, LAST_UNIT[BLOCKS[m - SPLIT_T]])
                nc.scalar.activation(wt_hi[:, m % SPLIT_T, :], raw_t[:, n % RAW_T, :], ACT.Copy).then_inc(w_hi_done, 1)

            def acc(u):
                act.wait_ge(acc_full, ACC.full(u))
                return bank[ACC.bank(u)]

            def tr(u):
                act.wait_ge(tr_full, TR.full(u))
                return bank[TR.bank(u)]

            def decay_tables():
                act.wait_ge(s_decay, 16)
                nc.scalar.activation(lgam[:], lgam[:], ACT.Exp).then_inc(s_exp, 1)
                act.wait_ge(s_lgam, 1)
                act.wait_ge(s_pow, 16)
                for h in range(H):
                    nc.scalar.activation(qfp[:, h, :], pows[:, 2, :], ACT.Exp, scale=lgam[:, 0, h:h + 1]).then_inc(s_tab, 1)
                    nc.scalar.activation(qbp[:, h, :], pows[:, 3, :], ACT.Exp, scale=lgam[:, 1, h:h + 1]).then_inc(s_tab, 1)
                act.wait_ge(s_lgam, 3)
                nc.scalar.activation(kdec[:], kdec[:], ACT.Exp).then_inc(s_tab, 1)
                nc.scalar.activation(cdec[:], lgam[:], ACT.Exp, scale=float(P)).then_inc(s_tab, 1)
                act.wait_ge(s_marg, 2 * H)
                nc.scalar.activation(mask[:], mask[:], ACT.Exp).then_inc(s_tab, 1)

            nc.scalar.activation(cols[:], tr(("vec", 0, 0))[:, 0:N_VEC], ACT.Copy).then_inc(tr_read["act"], 1)
            act.wait_ge(tr_read["act"], 1)
            nc.scalar.activation(scond[:], cols[:, 0:16].rearrange("p (a b) -> p a b", a=2), ACT.Silu).then_inc(s_scond, 1)
            act.wait_ge(s_scond, 1)
            nc.scalar.activation(sc_hi[:], scond[:], ACT.Copy).then_inc(s_scond, 1)
            split(0)
            for lt in range(NT):
                act.wait_ge(s_x[lt], 16)
                if lt:
                    act.wait_ge(s_ms, lt)
                nc.scalar.activation(x_sq[:], x_in[:, lt, :], ACT.Square, accum_out=small[:, lt:lt + 1]).then_inc(s_ms, 1)

            def ada_row(b):
                nc.scalar.activation(ada_row_sb[b >= 8][:, b % 2, :], acc(("ada", b, 0))[0:2, 0:256], ACT.Copy)\
                  .then_inc(acc_read["act"], 1)

            def normalise(lt):
                if lt >= 2:
                    act.wait_ge(tr_full, TR.full(("h", lt - 2, 1)))
                nc.scalar.activation(xn[:, lt % 2, :], x_in[:, lt, :], ACT.Copy, scale=small[:, 24 + lt:25 + lt])\
                  .then_inc(s_xn, 1)

            for b in range(8):
                split(b + 1)
                ada_row(b)
                if b == 4:
                    act.wait_ge(s_rstd, 1)
                    nc.scalar.activation(small[:, 16:21], small[:, 8:13], ACT.Sqrt).then_inc(s_sqrt, 1)
                    act.wait_ge(s_rstd, 2)
                    normalise(0)
                    normalise(1)
            def qk_out(s):
                kind, i = QKV[s // NT]
                src = acc((kind, i, s % NT))[:, 0:256]
                if s >= 2:
                    act.wait_ge(s_rope, s - 1)
                nc.scalar.activation(qk_raw[:, s % 2, :], src, ACT.Copy,
                                     scale=1.0 if kind == "q" else DK ** -0.5).then_inc(acc_read["act"], 1)
                if s >= 1:
                    qk_t(s - 1, tr)

            for lt in range(NT):
                if lt >= 1 and lt + 1 < NT:
                    normalise(lt + 1)
                for i in range(2):
                    z = 2 * lt + i
                    act.wait_ge(s_htmp, 4 * (z + 1))
                    nc.scalar.activation(act_hi[:, 4 * i:4 * i + 4, lt * P:(lt + 1) * P],
                                         h_tmp[:, z % 4, :].rearrange("p (a b) -> p a b", a=4), ACT.Copy).then_inc(s_hhi, 1)
                if lt == 3:
                    split(9)
                if lt:
                    qk_out(lt - 1)
            qk_out(NT - 1)
            for m in range(1, 8):
                kind, i = QKV[m]
                split(8 + m + 1)
                if m == 5:
                    decay_tables()
                for lt in range(NT):
                    if kind == "v":
                        nc.scalar.activation(v_n[:, lt, i * 256:(i + 1) * 256], acc((kind, i, lt))[:, 0:256], ACT.Copy)\
                          .then_inc(acc_read["act"], 1)
                    else:
                        qk_out(m * NT + lt)
                if m == 3:
                    qk_t(4 * NT - 1, tr)
            for h in range(H):
                if h:
                    on_t(h - 1, tr)
                for lt in range(NT + 1):
                    if lt:
                        src = acc(("o", h, lt - 1))[:, 0:DV]
                        if lt == 1 and h:
                            act.wait_ge(tr_full, TR.full(("on", h - 1, NT - 1)))
                        nc.scalar.activation(o_raw[:, lt - 1, :], src, ACT.Copy).then_inc(acc_read["act"], 1)
                    if lt < 4:
                        split(INDEX["ada", 8 + 4 * h + lt] + 1)
                        ada_row(8 + 4 * h + lt)
                act.wait_ge(s_mv, h + 1)
                nc.scalar.activation(small[:, 40:45], small[:, 32:37], ACT.Sqrt).then_inc(s_osq, 1)
            src = tr(("ada", 0, 0))
            nc.scalar.activation(adar[:], src[0:96, 0:P], ACT.Copy).then_inc(tr_read["act"], 1)
            act.wait_ge(tr_read["act"], TR_ACT["ada", 0, 0])
            nc.scalar.activation(small[:, 60:61], small[:, 24:25], ACT.Copy).then_inc(s_adar, 1)
            act.wait_ge(s_stdma, 16 * 2 * H)
            q = 0
            for m in range(32, 52):
                kind, i = BLOCKS[m]
                if kind == "wo":
                    break
                if kind == "sp" and i == 0:
                    for z in range(8):
                        act.wait_ge(s_gmul, 16 + z + 1)
                        g, f = z // 2, z % 2
                        nc.scalar.activation(py_hi[:, g, f * HALF:(f + 1) * HALF], rtmp[:, z % 2, :], ACT.Copy)\
                          .then_inc(s_ghi, 1)
                split(m + 1)
                if kind == "g" and i == 1:
                    on_t(H - 1, tr)
                for cc in range(4 if kind == "po" else 2):
                    for f in range(2):
                        span = slice(f * HALF, (f + 1) * HALF)
                        if kind == "g":
                            ct = 2 * i + cc
                            src = acc((kind, i, cc, f))[:, 0:HALF]
                            if q >= 2:
                                act.wait_ge(s_gmul, q - 1)
                            nc.scalar.activation(gtmp[:, q % 2, :], src, ACT.Silu).then_inc(acc_read["act"], 1)
                            act.wait_ge(s_gmul, q + 1)
                            nc.scalar.activation(ret_hi[:, ct, span], rtmp[:, q % 2, :], ACT.Copy).then_inc(s_ghi, 1)
                            q += 1
                        elif kind == "u":
                            ct = 2 * i + cc
                            src = acc((kind, i, cc, f))[:, 0:HALF]
                            nc.scalar.activation(pooled[:, ct, span], src, ACT.Copy).then_inc(acc_read["act"], 1)
                        elif kind in ("sr", "sp"):
                            ct = 2 * i + cc
                            src = acc((kind, i, cc, f))[:, 0:HALF]
                            if kind == "sr" and ct == 0:
                                act.wait_ge(s_gmul, 16)
                            dst, b0 = (mix, 8) if kind == "sr" else (sig_p, 0)
                            nc.scalar.activation(dst[:, ct, span], src, ACT.Sigmoid, bias=bbg[:, b0 + ct:b0 + ct + 1])\
                              .then_inc(acc_read["act"], 1)
                        elif kind == "po":
                            ct = 4 * i + cc
                            z = 2 * ct + f
                            act.wait_ge(s_gmul, 24 + z + 1)
                            nc.scalar.activation(act_hi[:, ct, span], rtmp[:, z % 2, :], ACT.Copy).then_inc(s_ghi, 1)
            for m in range(52, 56):
                split(m + 1)
            for lt in range(NT):
                act.wait_ge(s_x2, 3 * NT + lt + 1)
                tick(nc.scalar.activation(x2_sq[:], x2[:, lt, :], ACT.Square, accum_out=small[:, lt:lt + 1]))
                act.wait_ge(s_rstd, 3 + lt)
                nc.scalar.activation(small[:, 16 + lt:17 + lt], small[:, 8 + lt:9 + lt], ACT.Sqrt).then_inc(s_sqrt, 1)

            def e_split(e, n):
                act.wait_ge(e_landed[n % RAW_E], (e * (NB // RAW_E) + n // RAW_E + 1) * 16)
                act.wait_ge(e_used, e * NB + n + 1)
                nc.scalar.activation(we_hi[n % SPLIT_E][:], raw_e[:, n % RAW_E, :], ACT.Copy).then_inc(e_hi, 1)

            for lt in range(NT):
                for i in range(2):
                    if lt >= 2 and i == 0:
                        act.wait_ge(s_lg, lt - 1)
                    src = tr(("h2", lt, i))
                    nc.scalar.activation(h2_t[:, lt % 2, i * 512:(i + 1) * 512], src[:, :], ACT.Copy)\
                      .then_inc(tr_read["act"], 1)
                if lt == 1 or lt == 2:
                    e_split(0, lt - 1)
            act.wait_ge(s_rmax, 1)
            nc.scalar.activation(aff[:], aff[:], ACT.Exp).then_inc(s_rexp, 1)
            for i, n in ((0, L_S), (1, L_P)):
                src = tr(("af", i, 0))
                nc.scalar.activation(aff_t[:, 0, i * L_S:i * L_S + n], src[0:NE, 0:n], ACT.Copy).then_inc(tr_read["act"], 1)

            def tr_hi(e, g):
                act.wait_ge(e_tr, NG * (e + 1) + g + 1)
                dst, n = (xs_hi, 4) if g >= NJ else (hd_hi, TILE_EDGE[g % 4 + 1] - TILE_EDGE[g % 4])
                t0 = 4 * (g - NJ) if g >= NJ else FTH * (g // 4) + TILE_EDGE[g % 4]
                nc.scalar.activation(dst[:, t0:t0 + n, :], bank[5 + g % 2][:, 0:n * CAP].rearrange("p (a b) -> p a b", a=n),
                                     ACT.Copy).then_inc(e_tr_hi, 1 if not (isinstance(e, int) and e < 0 and g == NJ) else NJ + 1)

            tr_hi(-1, NJ)
            tr_hi(-1, NJ + 1)
            act.wait_ge(s_idx, 2)
            nc.scalar.activation(small[:, 61:62], small[:, 24:25], ACT.Copy).then_inc(e_silu, NJ)

            def expert(e, last):
                for n in range(NB):
                    if n + AHEAD < NB:
                        e_split(e, n + AHEAD)
                    elif not last:
                        e_split(e + 1, n + AHEAD - NB)
                    j = n // 2
                    if n < 2 * NJ and n % 2 == 0:
                        act.wait_ge(e_used, e * NB + n + 1 + SPLIT_E)
                        act.wait_ge(e_hid, NJ * e + NJ + j - 1)
                        nc.scalar.activation(silu_g[:, j % 2, :], bank[j % 2][0:CAP, 0:FB], ACT.Silu).then_inc(e_silu, 1)
                    if n in TR_AFTER:
                        g = TR_AFTER[n]
                        if g < NJ or not last:
                            tr_hi(e, g)

            with act.Fori(0, NE - 1) as e:
                expert(e, False)
            expert(NE - 1, True)
            for lt in range(NT):
                act.wait_ge(s_fin[lt], 16)
                tick(nc.scalar.activation(y_sq[:], y_tile[:, lt, :], ACT.Square, accum_out=small[:, lt:lt + 1]))
            act.wait_ge(s_rstd, 2 + NT + 1)
            nc.scalar.activation(small[:, 16:21], small[:, 8:13], ACT.Sqrt).then_inc(s_sqrt, 1)

        @block.vector
        def _(dve):
            steps = [0]

            def tick(ins):
                steps[0] += 1
                ins.then_inc(dve_step, 1)
                dve.wait_ge(dve_step, steps[0])

            def split(m):
                if m >= len(BLOCKS):
                    return
                n = m
                dve.wait_ge(w_hi_done, m + 1)
                nc.vector.tensor_tensor(wt_lo[:, m % SPLIT_T, :], raw_t[:, n % RAW_T, :],
                                        wt_hi[:, m % SPLIT_T, :].bitcast(F32), ALU.subtract).then_inc(w_lo_done, 1)

            def acc(u):
                dve.wait_ge(acc_full, ACC.full(u))
                return bank[ACC.bank(u)]

            def tr(u):
                dve.wait_ge(tr_full, TR.full(u))
                return bank[TR.bank(u)]

            def decay_tables():
                dve.wait_ge(s_exp, 1)
                nc.vector.tensor_scalar(lgam[:], lgam[:], -1.0, None, ALU.mult).then_inc(s_lgam, 1)
                dve.wait_ge(s_lgam, 1)
                dve.wait_ge(s_pow, 16)
                for d in range(2):
                    nc.vector.tensor_scalar(kdec[:, d, :], lgam[:, d, :], kpow[:, d:d + 1], None, ALU.mult).then_inc(s_lgam, 1)
                for h in range(H):
                    nc.vector.tensor_scalar(mask[:, h, :], pows[:, 0, :], lgam[:, 0, h:h + 1], None, ALU.mult).then_inc(s_marg, 1)
                dve.wait_ge(s_marg, H)
                for h in range(H):
                    nc.vector.scalar_tensor_tensor(out=mask[:, h, :], in0=pows[:, 1, :], scalar=lgam[:, 1, h:h + 1],
                                                   in1=mask[:, h, :], op0=ALU.mult, op1=ALU.add).then_inc(s_marg, 1)

            dve.wait_ge(tr_read["act"], 1)
            dve.wait_ge(s_scond, 2)
            nc.vector.tensor_tensor(sc_lo[:], scond[:], sc_hi[:].bitcast(F32), ALU.subtract).then_inc(s_scond, 1)
            split(0)
            for b in range(5):
                split(b + 1)
            dve.wait_ge(s_ms, NT)
            nc.vector.tensor_scalar(small[:, 8:13], small[:, 0:NT], 1.0 / D, EPS, ALU.mult, ALU.add).then_inc(s_rstd, 1)
            dve.wait_ge(s_sqrt, 1)
            nc.vector.reciprocal(small[:, 24:29], small[:, 16:21]).then_inc(s_rstd, 1)
            for b in range(5, 8):
                split(b + 1)
            dve.wait_ge(ada_done, 1)
            nc.vector.tensor_tensor(ada_t[:, 0:16, :], ada_ps[:, 0:32].rearrange("p (a b) -> p a b", b=2),
                                    bada[:, 0:16].unsqueeze(2).to_broadcast([P, 16, 2]), ALU.add).then_inc(s_ada0, 1)
            dve.wait_ge(s_ada0, 1)
            nc.vector.scalar_tensor_tensor(out=gs1[:], in0=ada_t[:, 8:16, :], scalar=1.0,
                                           in1=n1g.unsqueeze(2).to_broadcast([P, KT, 2]), op0=ALU.add, op1=ALU.mult)\
              .then_inc(s_gs, 1)
            dve.wait_ge(s_gs, 1)
            def rotate(s):
                kind, i = QKV[s // NT]
                lt = s % NT
                dve.wait_ge(acc_read["act"], 8 + s + 1)
                if kind == "q":
                    if s >= 2:
                        dve.wait_ge(tr_full, TR.full(("t",) + QKV[(s - 2) // NT] + ((s - 2) % NT,)))
                    dst = q_rope[:, s % 2, :]
                else:
                    dst = k_n[:, lt, i * 256:(i + 1) * 256]
                raw = qk_raw[:, s % 2, :]
                if lt == NS:
                    nc.vector.tensor_copy(dst, raw).then_inc(s_rope, 1)
                    return
                d2 = dst.rearrange("p (h d) -> p h d", h=2)
                r2 = raw.rearrange("p (h d) -> p h d", h=2)
                r4 = raw.rearrange("p (h d e) -> p h d e", h=2, e=2)
                s4 = sin_t[:, lt, :].rearrange("p (d e) -> p d e", e=2)
                tmp = rope_tmp[:, 0:256].rearrange("p (h d e) -> p h d e", h=2, e=2)
                if s:
                    dve.wait_ge(s_rope, s)
                nc.vector.tensor_tensor(d2, r2, cos_t[:, lt, :].unsqueeze(1).to_broadcast([P, 2, DK]), ALU.mult)\
                  .then_inc(dve_step, 1)
                nc.vector.tensor_tensor(tmp[:, :, :, 0], r4[:, :, :, 1], s4[:, :, 0].unsqueeze(1).to_broadcast([P, 2, 64]),
                                        ALU.mult).then_inc(dve_step, 1)
                nc.vector.tensor_tensor(tmp[:, :, :, 1], r4[:, :, :, 0], s4[:, :, 1].unsqueeze(1).to_broadcast([P, 2, 64]),
                                        ALU.mult).then_inc(dve_step, 1)
                steps[0] += 3
                dve.wait_ge(dve_step, steps[0])
                nc.vector.tensor_tensor(dst, dst, rope_tmp[:, 0:256], ALU.add).then_inc(s_rope, 1)

            dve.wait_ge(s_const, 16 * N_CONST)
            for lt in range(NT):
                cnd = int(lt == NS)
                for i in range(2):
                    z = 2 * lt + i
                    src = tr(("h", lt, i))
                    if z >= 4:
                        dve.wait_ge(s_hlo, z - 3)
                    for a in range(4):
                        k = 4 * i + a
                        nc.vector.tensor_scalar(h_tmp[:, z % 4, a * P:(a + 1) * P], src[:, a * P:(a + 1) * P],
                                                gs1[:, k, cnd:cnd + 1], ada_t[:, k, cnd:cnd + 1], ALU.mult, ALU.add)\
                          .then_inc(s_htmp, 1)
                if lt == 3:
                    split(9)
                if lt:
                    rotate(lt - 1)
            rotate(NT - 1)
            for m in range(1, 8):
                split(8 + m + 1)
                if m == 5:
                    decay_tables()
                if QKV[m][0] != "v":
                    for lt in range(NT):
                        rotate(m * NT + lt)
            dve.wait_ge(s_tab, 11)
            n_probs = 0
            for h in range(H):
                n_state = 6 * h
                for u in [("kvf", h, lt) for lt in (0, 1, 2)] + [("kvb", h, lt) for lt in (3, 2, 1)]:
                    d = int(u[0] == "kvb")
                    i = 3 - u[2] if d else u[2]
                    if i == 0:
                        dve.wait_ge(s_s0[h % 2], 32 * (h // 2 + 1))
                        before = s0[:, h % 2, d, :]
                    else:
                        dve.wait_ge(s_state, n_state)
                        before = states[:, 3 * d + i - 1, :]
                    src = acc(u)[:, 0:DV]
                    nc.vector.scalar_tensor_tensor(out=states[:, 3 * d + i, :], in0=before, scalar=cdec[:, d, h:h + 1],
                                                   in1=src, op0=ALU.mult, op1=ALU.add).then_inc(s_state, 1)
                    n_state += 1
                for d, name in ((0, "kvf"), (1, "kvb")):
                    if h:
                        dve.wait_ge(s_stdma, 16 * (2 * h))
                    src = acc((name, h, 4))[:, 0:DV]
                    nc.vector.tensor_copy(qk_raw[:, d, :], src).then_inc(acc_read["dve"], 1)
                for lt in range(NT):
                    src = acc(("sc", h, lt))[:, 0:P]
                    if n_probs >= 2:
                        ph, pl = divmod(n_probs - 2, NT)
                        dve.wait_ge(acc_full, ACC.full(("o", ph, pl)))
                    nc.vector.tensor_tensor(probs[:, n_probs % 2, :], src, mask[:, h, :], ALU.mult)\
                      .then_inc(acc_read["dve"], 1)
                    n_probs += 1
                    if lt < 4:
                        split(INDEX["ada", 8 + 4 * h + lt] + 1)
                for lt in range(NT):
                    dve.wait_ge(acc_read["act"], ACT_READ_O[h, lt])
                    tick(nc.vector.bn_stats(small[:, 52:58], o_raw[:, lt, :]))
                    tick(nc.vector.bn_aggr(mv[:, lt, :], small[:, 52:58]))
                nc.vector.tensor_scalar(small[:, 32:37], mv[:, :, 1], EPS, None, ALU.add).then_inc(s_mv, 1)
                dve.wait_ge(s_osq, h + 1)
                tick(nc.vector.reciprocal(small[:, 24:29], small[:, 40:45]))
                for lt in range(NT):
                    nc.vector.tensor_scalar(o_raw[:, lt, :], o_raw[:, lt, :], mv[:, lt, 0:1], small[:, 24 + lt:25 + lt],
                                            ALU.subtract, ALU.mult).then_inc(s_on, 1)
            dve.wait_ge(ada_done, 2)
            tick(nc.vector.tensor_tensor(ada_t[:, 16:48, :], ada_ps[:, 32:96].rearrange("p (a b) -> p a b", b=2),
                                         bada[:, 16:48].unsqueeze(2).to_broadcast([P, 32, 2]), ALU.add))
            nc.vector.scalar_tensor_tensor(out=ada_t[:, 32:40, :], in0=ada_t[:, 32:40, :], scalar=1.0,
                                           in1=n2g.unsqueeze(2).to_broadcast([P, KT, 2]), op0=ALU.add, op1=ALU.mult)\
              .then_inc(s_ada, 1)
            z = 0
            for m in range(32, 52):
                kind, i = BLOCKS[m]
                if kind == "sp" and i == 0:
                    for g in range(4):
                        for f in range(2):
                            span = slice(f * HALF, (f + 1) * HALF)
                            src = acc(("pg", g, f))[:, 0:HALF]
                            if z >= 2:
                                dve.wait_ge(s_glo, z - 1)
                            nc.vector.tensor_scalar(rtmp[:, z % 2, :], src, pscale[:, g:g + 1], None, ALU.mult)\
                              .then_inc(s_gmul, 1)
                            dve.wait_ge(s_ghi, z + 1)
                            nc.vector.tensor_tensor(py_lo[:, g, span], rtmp[:, z % 2, :],
                                                    py_hi[:, g, span].bitcast(F32), ALU.subtract).then_inc(s_glo, 1)
                            z += 1
                split(m + 1)
                for cc in range(4 if kind == "po" else 2):
                    for f in range(2):
                        span = slice(f * HALF, (f + 1) * HALF)
                        if kind == "g":
                            ct = 2 * i + cc
                            dve.wait_ge(acc_read["act"], ACT_READ_G[z])
                            dve.wait_ge(tr_read["act"], TR_READ_ON[i])
                            if z >= 2:
                                dve.wait_ge(s_glo, z - 1)
                            nc.vector.scalar_tensor_tensor(out=rtmp[:, z % 2, :], in0=o_t[:, ct, span],
                                                           scalar=gng[:, ct:ct + 1], in1=gtmp[:, z % 2, :],
                                                           op0=ALU.mult, op1=ALU.mult).then_inc(s_gmul, 1)
                            dve.wait_ge(s_ghi, z + 1)
                            nc.vector.tensor_tensor(ret_lo[:, ct, span], rtmp[:, z % 2, :],
                                                    ret_hi[:, ct, span].bitcast(F32), ALU.subtract).then_inc(s_glo, 1)
                            z += 1
                        elif kind == "ro":
                            ct = 2 * i + cc
                            src = acc((kind, i, cc, f))[:, 0:HALF]
                            dve.wait_ge(acc_read["act"], ACT_READ_SR)
                            nc.vector.tensor_tensor(mix[:, ct, span], src, mix[:, ct, span], ALU.mult)\
                              .then_inc(acc_read["dve"], 1)
                        elif kind == "po":
                            ct = 4 * i + cc
                            src = acc((kind, i, cc, f))[:, 0:HALF]
                            if z >= 2:
                                dve.wait_ge(s_glo, z - 1)
                            dve.wait_ge(acc_read["act"], ACT_READ_SP)
                            if ct == 0 and f == 0:
                                dve.wait_ge(acc_read["dve"], DVE_READ_RO)
                            nc.vector.tensor_tensor(rtmp[:, z % 2, :], src, sig_p[:, ct, span], ALU.mult)\
                              .then_inc(acc_read["dve"], 1)
                            dve.wait_ge(acc_read["dve"], DVE_READ[kind, i, cc, f])
                            nc.vector.tensor_tensor(rtmp[:, z % 2, :], rtmp[:, z % 2, :], mix[:, ct, span], ALU.add)\
                              .then_inc(s_gmul, 1)
                            z += 1
            dve.wait_ge(s_glo, z)
            nc.vector.tensor_copy(small[:, 61:62], kpow[:, 0:1]).then_inc(s_mixfree, 1)
            nc.vector.tensor_copy(small[:, 59:60], kpow[:, 0:1]).then_inc(e_lo, RAW_E)
            dve.wait_ge(s_bc, 64)

            def residual(i, lt):
                cnd = int(lt == NS)
                cs = slice(i * 256, (i + 1) * 256)
                src = acc(("wo", i, lt))[:, 0:256]
                if i == 0:
                    dve.wait_ge(s_x2in[lt], 16)
                tmp = rtmp[:, (NT * i + lt) % 2, 0:256]
                if NT * i + lt >= 2:
                    dve.wait_ge(s_x2, NT * i + lt - 1)
                nc.vector.tensor_tensor(tmp, src, g1_b[:, cnd, cs], ALU.mult).then_inc(acc_read["dve"], 1)
                dve.wait_ge(acc_read["dve"], DVE_READ["wo", i, lt])
                nc.vector.tensor_tensor(x2[:, lt, cs], x2[:, lt, cs], tmp, ALU.add).then_inc(s_x2, 1)

            def mean_square(lt):
                dve.wait_ge(act_step, lt + 1)
                nc.vector.tensor_scalar(small[:, 8 + lt:9 + lt], small[:, lt:lt + 1], 1.0 / D, EPS, ALU.mult, ALU.add)\
                  .then_inc(s_rstd, 1)

            def second_norm(lt):
                cnd = int(lt == NS)
                dve.wait_ge(s_sqrt, 2 + lt)
                tick(nc.vector.reciprocal(small[:, 24 + lt:25 + lt], small[:, 16 + lt:17 + lt]))
                if lt >= 3:
                    dve.wait_ge(s_h2w[lt - 3], 16)
                    dve.wait_ge(tr_full, TR.full(("h2", lt - 3, 1)))
                tick(nc.vector.scalar_tensor_tensor(out=h2[:, lt % 3, :], in0=x2[:, lt, :], scalar=small[:, 24 + lt:25 + lt],
                                                    in1=gs2_b[:, cnd, :], op0=ALU.mult, op1=ALU.mult))
                if lt == 0:
                    dve.wait_ge(s_sh2, 32)
                nc.vector.tensor_tensor(h2[:, lt % 3, :], h2[:, lt % 3, :], sh2_b[cnd][:], ALU.add).then_inc(s_h2, 1)

            for i in range(4):
                split(52 + i + 1)
                for lt in range(NT):
                    residual(i, lt)
                    if i == 3 and lt >= 2:
                        second_norm(lt - 2)
                    if i == 3 and lt >= 1:
                        mean_square(lt - 1)
            mean_square(NT - 1)
            second_norm(NT - 2)
            second_norm(NT - 1)

            def e_split(e, n):
                dve.wait_ge(e_hi, e * NB + n + 1)
                nc.vector.tensor_tensor(we_lo[n % SPLIT_E][:], raw_e[:, n % RAW_E, :],
                                        we_hi[n % SPLIT_E][:].bitcast(F32), ALU.subtract).then_inc(e_lo, 1)

            dve.wait_ge(s_h2, NT)
            for lt in range(NT):
                dve.wait_ge(s_lg, lt + 1)
                nc.vector.tensor_copy(lg_t[:, lt * P:(lt + 1) * P], bank[lt][0:NE, 0:P]).then_inc(s_lgt, 1)
                if lt == 1 or lt == 3:
                    e_split(0, lt // 2)
            dve.wait_ge(s_lg, NT + 1)
            nc.vector.tensor_copy(aff[:], bank[7][:, 0:NT * NE].rearrange("p (a b) -> p a b", a=NT)).then_inc(s_lg_rows, 1)
            dve.wait_ge(s_lg_rows, 1)
            tick(nc.vector.reduce_max(small[:, 48:48 + NT], aff[:], AX.X))
            nc.vector.tensor_tensor(aff[:], aff[:], small[:, 48:48 + NT].unsqueeze(2).to_broadcast([P, NT, NE]),
                                    ALU.subtract).then_inc(s_rmax, 1)
            dve.wait_ge(s_rexp, 1)
            tick(nc.vector.reduce_sum(small[:, 48:48 + NT], aff[:], AX.X))
            tick(nc.vector.reciprocal(small[:, 40:40 + NT], small[:, 48:48 + NT]))
            nc.vector.tensor_tensor(aff[:], aff[:], small[:, 40:40 + NT].unsqueeze(2).to_broadcast([P, NT, NE]),
                                    ALU.mult).then_inc(s_aff, 1)
            dve.wait_ge(tr_read["act"], TR_READ_AF)
            for lo, n, cap, c0 in ((0, L_S, C_S, 0), (L_S, L_P, C_P, C_S)):
                src = 0
                for r in range(cap // 8):
                    o = slice(c0 + 8 * r, c0 + 8 * r + 8)
                    cur = aff_t[:, src, lo:lo + n]
                    tick(nc.vector.max(top_v[:, o], cur))
                    nc.vector.max_index(top_i[:, o], top_v[:, o], cur).then_inc(s_top, 1)
                    if r + 1 < cap // 8:
                        tick(nc.vector.match_replace(out=aff_t[:, 1 - src, lo:lo + n], in_to_replace=top_v[:, o],
                                                     in_values=cur, imm_value=-1.0))
                        src = 1 - src
            dve.wait_ge(s_top, CAP // 8)
            tick(nc.vector.tensor_copy(top_f[:], top_i[:]))
            nc.vector.tensor_scalar(top_f[:, C_S:CAP], top_f[:, C_S:CAP], float(L_S), None, ALU.add).then_inc(s_top, 1)
            src = tr(("ix", 0, 0))
            nc.vector.tensor_copy(idx_all[:], src[0:CAP, 0:NE]).then_inc(s_idx, 1)
            dve.wait_ge(s_idx, 1)
            nc.vector.tensor_copy(idx_gather[:], idx_all[:, 0:1]).then_inc(e_idx, 1)
            src = tr(("ga", 0, 0))
            nc.vector.tensor_copy(gate_all[:], src[0:CAP, 0:NE]).then_inc(s_idx, 1)
            dve.wait_ge(s_idx, 2)

            def tr_lo(e, g, inc=1):
                dve.wait_ge(e_tr_hi, NG * (e + 1) + g + 1)
                hi, lo, n = (xs_hi, xs_lo, 4) if g >= NJ else (hd_hi, hd_lo, TILE_EDGE[g % 4 + 1] - TILE_EDGE[g % 4])
                t0 = 4 * (g - NJ) if g >= NJ else FTH * (g // 4) + TILE_EDGE[g % 4]
                nc.vector.tensor_tensor(lo[:, t0:t0 + n, :], bank[5 + g % 2][:, 0:n * CAP].rearrange("p (a b) -> p a b", a=n),
                                        hi[:, t0:t0 + n, :].bitcast(F32), ALU.subtract).then_inc(e_tr_split, inc)

            tr_lo(-1, NJ, NJ + 1)
            tr_lo(-1, NJ + 1)
            nc.vector.tensor_copy(small[:, 58:59], kpow[:, 0:1]).then_inc(e_hid, NJ)
            nc.vector.tensor_copy(small[:, 57:58], kpow[:, 0:1]).then_inc(e_out, NQ)
            dve.wait_ge(s_g2, 32)

            def expert(e, last):
                if not last:
                    dve.wait_ge(e_gath, 16 * e + 16)
                    nc.vector.tensor_copy(idx_gather[:], idx_all[:, bass.ds(e + 1, 1)]).then_inc(e_idx, 1)
                for n in range(NB):
                    if n + AHEAD < NB:
                        e_split(e, n + AHEAD)
                    elif not last:
                        e_split(e + 1, n + AHEAD - NB)
                    j = n // 2
                    if n < 2 * NJ and n % 2:
                        dve.wait_ge(e_used, e * NB + n + 1 + SPLIT_E)
                        dve.wait_ge(e_silu, NJ * e + NJ + j + 1)
                        g = j - 3 - (j % 4 == 3)
                        dve.wait_ge(e_tr, NG * e + (NG + g + 1 if g >= 0 else NJ + g + 1))
                        nc.vector.tensor_tensor(hid[:, (j % 4) * FB:(j % 4 + 1) * FB], silu_g[:, j % 2, :],
                                                bank[2 + j % 2][0:CAP, 0:FB], ALU.mult).then_inc(e_hid, 1)
                    if n == 1:
                        dve.wait_ge(s_acc, 16 * NT + 16 * e)
                        col = slice(e, e + 1) if isinstance(e, int) else bass.ds(e, 1)
                        nc.vector.tensor_copy(idx_scatter[:], idx_all[:, col]).then_inc(e_idx, 1)
                        nc.vector.tensor_copy(gate_cur[:], gate_all[:, col]).then_inc(s_idx, 1)
                    if n in TR_AFTER:
                        g = TR_AFTER[n]
                        if g < NJ or not last:
                            tr_lo(e, g)
                    if n >= 2 * NJ and n % 2:
                        q = (n - 2 * NJ) // 2
                        dve.wait_ge(e_used, e * NB + n + 1 + SPLIT_E)
                        if q == 0:
                            dve.wait_ge(s_idx, e + 3)
                        nc.vector.scalar_tensor_tensor(
                            out=out_rows[:, q * DQ:(q + 1) * DQ], in0=bank[DOWN_BANK[q % 2]][0:CAP, 0:DQ],
                            scalar=gate_cur[:, 0:1], in1=g2_rows[:, q * DQ:(q + 1) * DQ],
                            op0=ALU.mult, op1=ALU.mult).then_inc(e_out, 1)

            with dve.Fori(0, NE - 1) as e:
                expert(e, False)
            expert(NE - 1, True)
            dve.wait_ge(s_fg, 16)
            dve.wait_ge(act_step, 2 * NT)
            nc.vector.tensor_scalar(small[:, 8:13], small[:, 0:NT], 1.0 / D, EPS, ALU.mult, ALU.add).then_inc(s_rstd, 1)
            dve.wait_ge(s_sqrt, 1 + NT + 1)
            tick(nc.vector.reciprocal(small[:, 24:29], small[:, 16:21]))
            for lt in range(NT):
                nc.vector.scalar_tensor_tensor(out=y_tile[:, lt, :], in0=y_tile[:, lt, :], scalar=small[:, 24 + lt:25 + lt],
                                               in1=fg_b[:], op0=ALU.mult, op1=ALU.mult).then_inc(s_y, 1)

        @block.tensor
        def _(pe):
            mm = nc.tensor.matmul

            def acc(u):
                before = ACC.previous(u)
                if before:
                    pe.wait_ge(acc_read[before[0]], before[1])
                return bank[ACC.bank(u)]

            def tr(u):
                before = TR.previous(u)
                if before:
                    pe.wait_ge(tr_read[before[0]], before[1])
                return bank[TR.bank(u)]

            def transpose(dst, src):
                n = src.shape[0]
                return nc.tensor.transpose(dst, src, ident[0:n, 0:n])

            def ada(b):
                n = INDEX["ada", b]
                pe.wait_ge(w_lo_done, n + 1)
                wh = wt_hi[:, n % SPLIT_T, :].rearrange("p (k f) -> p k f", k=KT)
                wl = wt_lo[:, n % SPLIT_T, :].rearrange("p (k f) -> p k f", k=KT)
                pairs = [pr for k in range(KT) for pr in ((sc_hi[:, :, k], wh[:, k, :]), (sc_lo[:, :, k], wh[:, k, :]),
                                                           (sc_hi[:, :, k], wl[:, k, :]))]
                three(acc(("ada", b, 0))[0:2, 0:256], pairs, 3 * KT).then_inc(acc_full, 1)
                if b % 8:
                    ada_channels(b - 1)

            def ada_channels(b):
                pe.wait_ge(acc_read["act"], ACT_READ["ada", b, 0])
                for j in range(2):
                    c0 = 2 * (2 * b + j)
                    ins = transpose(ada_ps[:, c0:c0 + 2], ada_row_sb[b >= 8][:, b % 2, j * P:(j + 1) * P])
                if b in (7, 23):
                    ins.then_inc(ada_done, 1)

            def three(out, pairs, count):
                i = 0
                for a, b in pairs:
                    ins = mm(out, a, b, start=i == 0, stop=i == count - 1)
                    i += 1
                return ins

            def by_tokens(b, hi, lo, after=None):
                m = INDEX[b]
                pe.wait_ge(w_lo_done, m + 1)
                wh = wt_hi[:, m % SPLIT_T, :].rearrange("p (k f) -> p k f", k=KT)
                wl = wt_lo[:, m % SPLIT_T, :].rearrange("p (k f) -> p k f", k=KT)
                for lt in range(NT):
                    if b == ("q", 0):
                        if lt + 1 < NT:
                            h_transpose(lt + 1)
                        pe.wait_ge(s_hlo, 2 * lt + 2)
                    o = acc(b + (lt,))[:, 0:256]
                    sl = slice(lt * P, (lt + 1) * P)
                    pairs = [pr for k in range(KT) for pr in ((hi[:, k, sl], wh[:, k, :]), (lo[:, k, sl], wh[:, k, :]),
                                                               (hi[:, k, sl], wl[:, k, :]))]
                    three(o, pairs, 3 * KT).then_inc(acc_full, 1)
                    if after:
                        after(lt)
                return m

            def by_channels(b, hi, lo, kts, width):
                m = INDEX[b]
                pe.wait_ge(w_lo_done, m + 1)
                wh = wt_hi[:, m % SPLIT_T, :].rearrange("p (k f) -> p k f", k=kts)
                wl = wt_lo[:, m % SPLIT_T, :].rearrange("p (k f) -> p k f", k=kts)
                for cc in range(width // P):
                    cs = slice(cc * P, (cc + 1) * P)
                    for f in range(2):
                        o = acc(b + (cc, f))[:, 0:HALF]
                        fs = slice(f * HALF, (f + 1) * HALF)
                        pairs = [pr for k in range(kts) for pr in (
                            (wh[:, k, cs], hi[:, k, fs]), (wh[:, k, cs], lo[:, k, fs]), (wl[:, k, cs], hi[:, k, fs]))]
                        three(o, pairs, 3 * kts).then_inc(acc_full, 1)

            pe.wait_ge(s_cond, 16 * 9)
            transpose(tr(("vec", 0, 0))[:, 0:N_VEC], vec_rows[:]).then_inc(tr_full, 1)
            pe.wait_ge(s_scond, 3)
            for b in range(8):
                ada(b)
            ada_channels(7)
            def h_transpose(lt):
                pe.wait_ge(s_xn, lt + 1)
                for i in range(2):
                    o = tr(("h", lt, i))
                    for a in range(4):
                        k = 4 * i + a
                        ins = transpose(o[:, a * P:(a + 1) * P], xn[:, lt % 2, k * P:(k + 1) * P])
                    ins.then_inc(tr_full, 1)

            h_transpose(0)

            def qk_transpose(s):
                kind, i = QKV[s // NT]
                lt = s % NT
                pe.wait_ge(s_rope, s + 1)
                o = tr(("t", kind, i, lt))
                for a in range(2):
                    src = q_rope[:, s % 2, a * P:(a + 1) * P] if kind == "q" else k_n[:, lt, i * 256 + a * P:i * 256 + (a + 1) * P]
                    ins = transpose(o[:, a * P:(a + 1) * P], src)
                ins.then_inc(tr_full, 1)

            for m in range(8):
                b = QKV[m]

                def after(lt, m=m):
                    s = m * NT + lt - 1
                    if 0 <= s < 4 * NT and m < 4:
                        qk_transpose(s)

                by_tokens(b, act_hi, act_lo, after if m < 4 else None)
                if m == 3:
                    qk_transpose(4 * NT - 1)

            def on_transpose(h):
                for lt in range(NT):
                    pe.wait_ge(s_on, NT * h + lt + 1)
                    o = tr(("on", h, lt))
                    for a in range(2):
                        ins = transpose(o[:, a * P:(a + 1) * P], o_raw[:, lt, a * P:(a + 1) * P])
                    ins.then_inc(tr_full, 1)

            pe.wait_ge(acc_read["act"], 8 + 8 * NT)
            pe.wait_ge(tr_read["act"], 4 * NT + 1)
            pe.wait_ge(s_ada0, 1)
            for h in range(H):
                pe.wait_ge(s_kdec, 2 * h + 2)
                for u in [("kvf", h, lt) for lt in (0, 1, 2)] + [("kvb", h, lt) for lt in (3, 2, 1)] + [("kvf", h, 4), ("kvb", h, 4)]:
                    lt = u[2]
                    k = (kb if u[0] == "kvb" else kf)[:, lt, :]
                    o = acc(u)[:, 0:DV]
                    mm(o, k, v_n[:, lt, h * DV:(h + 1) * DV], start=True, stop=True).then_inc(acc_full, 1)
                if h:
                    on_transpose(h - 1)
                pe.wait_ge(s_qdec, 2 * h + 2)
                pe.wait_ge(s_state, 6 * h + 6)
                for lt in range(NT + 1):
                    if lt < NT:
                        sl = slice(lt * P, (lt + 1) * P)
                        mm(acc(("sc", h, lt))[:, 0:P], k_t[:, h, sl], q_t[:, h, sl], start=True, stop=True).then_inc(acc_full, 1)
                    if lt:
                        t = lt - 1
                        o = acc(("o", h, t))[:, 0:DV]
                        pe.wait_ge(acc_read["dve"], DVE_READ["sc", h, t])
                        ins = mm(o, probs[:, (NT * h + t) % 2, :], v_n[:, t, h * DV:(h + 1) * DV], start=True, stop=t == NS)
                        if t < NS:
                            mm(o, qf[:, t, :], s0[:, h % 2, 0, :] if t == 0 else states[:, t - 1, :], start=False, stop=False)
                            ins = mm(o, qb[:, t, :], s0[:, h % 2, 1, :] if t == 3 else states[:, 3 + 2 - t, :],
                                     start=False, stop=True)
                        ins.then_inc(acc_full, 1)
                    if lt < 4:
                        ada(8 + 4 * h + lt)
                if h % 2:
                    ada_channels(11 + 4 * h)
            pe.wait_ge(s_ada, 1)
            transpose(tr(("ada", 0, 0))[0:96, 0:P], ada_t[:].rearrange("p a b -> p (a b)")).then_inc(tr_full, 1)
            for m in range(32, 52):
                b = BLOCKS[m]
                kind, i = b
                if b == ("ro", 0):
                    pe.wait_ge(s_glo, 16)
                if b == ("sp", 0):
                    pe.wait_ge(s_pooled, 1)
                    pe.wait_ge(s_const, 16 * N_CONST)
                    for g in range(4):
                        for f in range(2):
                            mm(acc(("pg", g, f))[:, 0:HALF], wp_sb[:, g, :], pooled[:, g, f * HALF:(f + 1) * HALF],
                               start=True, stop=True).then_inc(acc_full, 1)
                if b == ("po", 0):
                    pe.wait_ge(s_glo, 24)
                hi, lo = {"ro": (ret_hi, ret_lo), "po": (py_hi, py_lo)}.get(kind, (act_hi, act_lo))
                by_channels(b, hi, lo, 4 if kind == "po" else KT, 512 if kind == "po" else 256)
                if b == ("g", 0):
                    on_transpose(H - 1)
            pe.wait_ge(s_glo, 40)
            for i in range(4):
                by_tokens(("wo", i), act_hi, act_lo)
            def h2_transpose(lt):
                pe.wait_ge(s_h2, lt + 1)
                for i in range(2):
                    o = tr(("h2", lt, i))
                    for a in range(4):
                        k = 4 * i + a
                        ins = transpose(o[:, a * P:(a + 1) * P], h2[:, lt % 3, k * P:(k + 1) * P])
                        if k == 0 and lt == 0:
                            ins.then_inc(e_used, SPLIT_E)
                    ins.then_inc(tr_full, 1)

            h2_transpose(0)
            pe.wait_ge(acc_read["dve"], DVE_READ["wo", 3, NT - 1])
            pe.wait_ge(s_const, 16 * N_CONST)
            for lt in range(NT):
                if lt + 1 < NT:
                    h2_transpose(lt + 1)
                pe.wait_ge(tr_read["act"], TR_READ_H2[lt])
                for k in range(KT):
                    ins = mm(bank[lt][0:NE, 0:P], wr_sb[:, k, :], h2_t[:, lt % 2, k * P:(k + 1) * P],
                             start=k == 0, stop=k == KT - 1)
                ins.then_inc(s_lg, 1)
            pe.wait_ge(s_lgt, NT)
            for lt in range(NT):
                ins = transpose(bank[7][:, lt * NE:(lt + 1) * NE], lg_t[:, lt * P:(lt + 1) * P])
            ins.then_inc(s_lg, 1)
            pe.wait_ge(s_aff, 1)
            for i, tiles in ((0, range(NS)), (1, (NS,))):
                o = tr(("af", i, 0))
                for lt in tiles:
                    ins = transpose(o[0:NE, (lt % NS) * P:(lt % NS + 1) * P], aff[:, lt, :])
                ins.then_inc(tr_full, 1)
            pe.wait_ge(s_top, CAP // 8 + 1)
            transpose(tr(("ix", 0, 0))[0:CAP, 0:NE], top_f[:]).then_inc(tr_full, 1)
            transpose(tr(("ga", 0, 0))[0:CAP, 0:NE], top_v[:]).then_inc(tr_full, 1)

            def group(e, g):
                if g >= NJ:
                    pe.wait_ge(e_gath, 16 * e + 32)
                else:
                    pe.wait_ge(e_hid, NJ * e + NJ + g + 1)
                if not (isinstance(e, int) and e < 0):
                    pe.wait_ge(e_tr_split, NG * e + NG + g - 1)
                n = 4 if g >= NJ else TILE_EDGE[g % 4 + 1] - TILE_EDGE[g % 4]
                for i in range(n):
                    t = 4 * (g - NJ) + i if g >= NJ else TILE_EDGE[g % 4] + i
                    src = (x_rows if g >= NJ else hid)[:, t * P:(t + 1) * P]
                    ins = transpose(bank[5 + g % 2][:, i * CAP:(i + 1) * CAP], src)
                ins.then_inc(e_tr, NJ + 1 if isinstance(e, int) and e < 0 and g == NJ else 1)

            pe.wait_ge(s_idx, 2)
            group(-1, NJ)
            group(-1, NJ + 1)

            def expert(e, last):
                for n in range(NB):
                    j = n // 2
                    pe.wait_ge(e_lo, e * NB + n + 1 + RAW_E)
                    wh, wl = we_hi[n % SPLIT_E][:], we_lo[n % SPLIT_E][:]
                    if n < 2 * NJ:
                        if n == 0:
                            pe.wait_ge(e_tr_split, NG * e + NG)
                        if n % 2 == 0:
                            pe.wait_ge(e_silu, NJ * e + NJ + j - 1)
                        else:
                            pe.wait_ge(e_hid, NJ * e + NJ + j - 1)
                        o = bank[2 * (n % 2) + j % 2][0:CAP, 0:FB]
                        wh, wl = (w.rearrange("p (k f) -> p k f", k=KT) for w in (wh, wl))
                        pairs = [pr for k in range(KT) for pr in (
                            (xs_hi[:, k, :], wh[:, k, :]), (xs_lo[:, k, :], wh[:, k, :]), (xs_hi[:, k, :], wl[:, k, :]))]
                        three(o, pairs, 3 * KT).then_inc(e_used, 1)
                    else:
                        q, part = (n - 2 * NJ) // 2, n % 2
                        if part == 0:
                            pe.wait_ge(e_out, NQ * e + NQ + q - 1)
                        if q == 0:
                            pe.wait_ge(e_tr_split, NG * e + NG + 4 + 4 * part)
                        o = bank[DOWN_BANK[q % 2]][0:CAP, 0:DQ]
                        wh, wl = (w.rearrange("p (k f) -> p k f", k=FTH) for w in (wh, wl))
                        for i in range(FTH):
                            t = part * FTH + i
                            for z, (a, b) in enumerate(((hd_hi, wh), (hd_lo, wh), (hd_hi, wl))):
                                ins = mm(o, a[:, t, :], b[:, i, :], start=t == 0 and z == 0, stop=t == FT - 1 and z == 2)
                        ins.then_inc(e_used, 1)
                    if n in TR_AFTER:
                        g = TR_AFTER[n]
                        if g < NJ or not last:
                            group(e, g)

            with pe.Fori(0, NE - 1) as e:
                expert(e, False)
            expert(NE - 1, True)


DOWN_BANK = (4, 7)
TR_AFTER = {**{2 * g + 2: g for g in range(NJ)}, 2 * NJ + 3: NJ, 2 * NJ + 4: NJ + 1}
N_CONST = 6
N_VEC = 108


def _counts(units, engine):
    out, n = {}, 0
    for u, e in units:
        if e == engine:
            n += 1
            out[u] = n
    return out


LAST_UNIT = {b: max(ACC.full(u) for u in ACC.at if u[:2] == b and len(u) > 2) for b in BLOCKS}
ACT_READ = _counts(acc_units(), "act")
DVE_READ = _counts(acc_units(), "dve")
TR_ACT = _counts(tr_units(), "act")
ACT_READ_U = [ACT_READ["u", g // 2, g % 2, 1] for g in range(4)]
ACT_READ_O = {(h, lt): ACT_READ["o", h, lt] for h in range(H) for lt in range(NT)}
ACT_READ_G = [ACT_READ["g", z // 4, z // 2 % 2, z % 2] for z in range(16)]
ACT_READ_SR = ACT_READ["sr", 3, 1, 1]
ACT_READ_SP = ACT_READ["sp", 3, 1, 1]
DVE_READ_RO = DVE_READ["ro", 3, 1, 1]
TR_READ_ON = [TR_ACT["on", h, NT - 1] for h in range(H)]
TR_READ_AF = TR_ACT["af", 1, 0]
TR_READ_H2 = [TR_ACT["h2", lt, 1] for lt in range(NT)]


_INS = ["x_prompt", "x_sample", "c", "state_ret", "c_ctx", "w_ada", "b_ada", "norm1_g", "w_in", "w_pool", "pool_scale",
        "w_pool_out", "ret_decay", "ret_gn_g", "w_ret_out", "w_branch_gate", "b_branch_gate", "w_out", "norm2_g",
        "w_router", "w_exp_gate", "w_exp_up", "w_exp_down", "final_norm_g"]
_OUTS = [(1, L_P, D), (1, L_S, D), (1, 1, 2, H, DK, DV)]


def kernel(**inputs):
    import concourse.bacc as bacc
    from concourse.bass_utils import run_bass_kernel_spmd as run

    nc = bacc.Bacc("TRN2", target_bir_lowering=False, num_devices=1)
    arrays, args = {}, []
    for name in _INS:
        a = np.ascontiguousarray(inputs[name])
        arrays[f"in_{name}_dram"] = a
        args.append(nc.dram_tensor(f"in_{name}_dram", a.shape, mybir.dt.from_np(a.dtype), kind="ExternalInput").ap())
    arrays["tables_dram"] = shape_tables()
    args.append(nc.dram_tensor("tables_dram", (P, C_END), F32, kind="ExternalInput").ap())
    for i, shape in enumerate(_OUTS):
        args.append(nc.dram_tensor(f"out_{i}_dram", shape, F32, kind="ExternalOutput").ap())
    build(nc, *args)
    r = run(nc, [arrays], core_ids=[0])
    return tuple(r.results[0][f"out_{i}_dram"] for i in range(len(_OUTS)))
```
